# Optimizing a Trainium2 kernel written in Bass

```python
import math
import jax, jax.numpy as jnp
from jax import lax
import numpy as np

D_MODEL = 2048
BATCH = 1
SEQ = 256
DEPTH = 1

N_META = 16
BLOCK = 128
PAD = BLOCK - N_META

ATT_WIDTH = D_MODEL // 2
ATT_HEAD_DIM = 64
ATT_Q_HEADS = ATT_WIDTH // ATT_HEAD_DIM
ATT_KV_HEADS = 2
ATT_GROUP = ATT_Q_HEADS // ATT_KV_HEADS
ATT_KV_WIDTH = ATT_KV_HEADS * ATT_HEAD_DIM
WINDOW = 128
ROPE_THETA = 10000.0

RET_WIDTH = D_MODEL - ATT_WIDTH
RET_HEAD_DIM = 256
RET_HEADS = RET_WIDTH // RET_HEAD_DIM

MIX_WIDTH = ATT_WIDTH + RET_WIDTH
SPLITS = [ATT_WIDTH,
          ATT_WIDTH + ATT_KV_WIDTH,
          ATT_WIDTH + 2 * ATT_KV_WIDTH,
          ATT_WIDTH + 2 * ATT_KV_WIDTH + RET_WIDTH,
          ATT_WIDTH + 2 * ATT_KV_WIDTH + 2 * RET_WIDTH,
          ATT_WIDTH + 2 * ATT_KV_WIDTH + 3 * RET_WIDTH]
IN_COLS = ATT_WIDTH + 2 * ATT_KV_WIDTH + 4 * RET_WIDTH

PEER_HEADS = 8
PEER_N_KEYS = 128
PEER_N_EXPERTS = PEER_N_KEYS * PEER_N_KEYS
PEER_D_KEY = 256
PEER_HALF = PEER_D_KEY // 2
PEER_TOPK = 16
PEER_TOKEN_BLOCK = 128

DEEPNORM_ALPHA = (2 * DEPTH) ** 0.25
DEEPNORM_BETA = (8 * DEPTH) ** -0.25
LN_EPS = 1e-5
GN_EPS = 1e-5
NEG = -1e30

kernel_name = "hymba_swa_sink_retnet_peer_deepnorm"

def layer_norm(x, g, b):
    xf = x.astype(jnp.float32)
    mu = jnp.mean(xf, axis=-1, keepdims=True)
    var = jnp.mean(jnp.square(xf - mu), axis=-1, keepdims=True)
    y = (xf - mu) * lax.rsqrt(var + LN_EPS) * g.astype(jnp.float32) + b.astype(jnp.float32)
    return y.astype(x.dtype)

def rope(t, pos):
    dh = t.shape[-1]
    inv = ROPE_THETA ** (-jnp.arange(0, dh, 2, dtype=jnp.float32) / dh)
    ang = pos.astype(jnp.float32)[:, None] * inv[None, :]
    cos = jnp.cos(ang)[None, :, None, :]
    sin = jnp.sin(ang)[None, :, None, :]
    tf = t.astype(jnp.float32)
    t1, t2 = tf[..., : dh // 2], tf[..., dh // 2:]
    return jnp.concatenate([t1 * cos - t2 * sin, t2 * cos + t1 * sin], axis=-1).astype(t.dtype)

def sliding_window_attention(q, k, v, sinks):
    B, Lp = q.shape[0], q.shape[1]
    nb = Lp // BLOCK
    qb = q.reshape(B, nb, BLOCK, ATT_KV_HEADS, ATT_GROUP, ATT_HEAD_DIM).astype(jnp.float32)

    def with_prev(t):
        tb = t.reshape(B, nb, BLOCK, ATT_KV_HEADS, ATT_HEAD_DIM).astype(jnp.float32)
        prev = jnp.concatenate([jnp.zeros_like(tb[:, :1]), tb[:, :-1]], axis=1)
        return jnp.concatenate([prev, tb], axis=2)

    kb, vb = with_prev(k), with_prev(v)
    scores = jnp.einsum('bnqhgd,bnkhd->bnhgqk', qb, kb) * (ATT_HEAD_DIM ** -0.5)
    blk = jnp.arange(nb)[:, None] * BLOCK
    qpos = blk + jnp.arange(BLOCK)[None, :]
    kpos = blk - BLOCK + jnp.arange(2 * BLOCK)[None, :]
    diff = qpos[:, :, None] - kpos[:, None, :]
    mask = (diff >= 0) & (diff < WINDOW) & (kpos[:, None, :] >= PAD)
    scores = jnp.where(mask[None, :, None, None], scores, NEG)
    sink = sinks.astype(jnp.float32).reshape(1, 1, ATT_KV_HEADS, ATT_GROUP, 1, 1)
    m = jnp.maximum(jnp.max(scores, axis=-1, keepdims=True), sink)
    p = jnp.exp(scores - m)
    denom = jnp.sum(p, axis=-1, keepdims=True) + jnp.exp(sink - m)
    p = p / denom
    out = jnp.einsum('bnhgqk,bnkhd->bnqhgd', p, vb)
    return out.reshape(B, Lp, ATT_Q_HEADS * ATT_HEAD_DIM).astype(q.dtype)

def chunkwise_retention(q, k, v):
    B, Lp = q.shape[0], q.shape[1]
    nb = Lp // BLOCK
    log_gamma = jnp.log(1.0 - 2.0 ** (-5.0 - jnp.arange(RET_HEADS, dtype=jnp.float32)))
    idx = jnp.arange(BLOCK, dtype=jnp.float32)
    rel = idx[:, None] - idx[None, :]
    inner_decay = jnp.where(rel[None] >= 0,
                            jnp.exp(jnp.maximum(rel, 0.0)[None] * log_gamma[:, None, None]), 0.0)
    q_decay = jnp.exp((idx[None, :] + 1.0) * log_gamma[:, None])[:, :, None]
    k_decay = jnp.exp((BLOCK - 1.0 - idx[None, :]) * log_gamma[:, None])[:, :, None]
    chunk_decay = jnp.exp(BLOCK * log_gamma)[:, None, None]

    def to_chunks(t):
        return t.astype(jnp.float32).reshape(B, nb, BLOCK, RET_HEADS, t.shape[-1]).transpose(1, 0, 3, 2, 4)

    qs, ks, vs = to_chunks(q), to_chunks(k * (RET_HEAD_DIM ** -0.5)), to_chunks(v)

    def step(state, inp):
        qc, kc, vc = inp
        att = jnp.einsum('bhid,bhjd->bhij', qc, kc) * inner_decay
        o = jnp.einsum('bhij,bhje->bhie', att, vc) + jnp.einsum('bhid,bhde->bhie', qc * q_decay, state)
        state = state * chunk_decay + jnp.einsum('bhjd,bhje->bhde', kc * k_decay, vc)
        return state, o

    state0 = jnp.zeros((B, RET_HEADS, RET_HEAD_DIM, v.shape[-1]), jnp.float32)
    _, o = lax.scan(step, state0, (qs, ks, vs))
    return o.transpose(1, 0, 3, 2, 4).reshape(B, Lp, RET_HEADS, v.shape[-1])

def hybrid_mixer(h, w_in, sinks, w_out, pos, key_valid):
    B, Lp, _ = h.shape
    proj = h @ w_in
    aq, ak, av, rq, rk, rv, rg = jnp.split(proj, SPLITS, axis=-1)
    aq = rope(aq.reshape(B, Lp, ATT_Q_HEADS, ATT_HEAD_DIM), pos)
    ak = rope(ak.reshape(B, Lp, ATT_KV_HEADS, ATT_HEAD_DIM), pos)
    av = av.reshape(B, Lp, ATT_KV_HEADS, ATT_HEAD_DIM)
    att_out = sliding_window_attention(aq, ak, av, sinks)
    rq = rope(rq.reshape(B, Lp, RET_HEADS, RET_HEAD_DIM), pos)
    rk = rope((rk * key_valid).reshape(B, Lp, RET_HEADS, RET_HEAD_DIM), pos)
    rv = rv.reshape(B, Lp, RET_HEADS, RET_HEAD_DIM)
    ret = chunkwise_retention(rq, rk, rv)
    mu = jnp.mean(ret, axis=-1, keepdims=True)
    var = jnp.mean(jnp.square(ret - mu), axis=-1, keepdims=True)
    ret = ((ret - mu) * lax.rsqrt(var + GN_EPS)).reshape(B, Lp, RET_WIDTH)
    ret_out = (jax.nn.silu(rg.astype(jnp.float32)) * ret).astype(h.dtype)
    mixed = jnp.concatenate([att_out, ret_out], axis=-1)
    return mixed @ w_out

def peer(h, wq, subkeys, u_tab, v_tab):
    B, Lp, D = h.shape
    T = B * Lp
    t = h.reshape(T, D)
    q = (t @ wq).reshape(T, PEER_HEADS, 2, PEER_HALF).astype(jnp.float32)
    s = jnp.einsum('thpc,hpnc->thpn', q, subkeys.astype(jnp.float32))
    sv, si = lax.top_k(s, PEER_TOPK)
    cand = (sv[:, :, 0, :, None] + sv[:, :, 1, None, :]).reshape(T, PEER_HEADS, PEER_TOPK * PEER_TOPK)
    fv, fi = lax.top_k(cand, PEER_TOPK)
    i1 = jnp.take_along_axis(si[:, :, 0], fi // PEER_TOPK, axis=-1)
    i2 = jnp.take_along_axis(si[:, :, 1], fi % PEER_TOPK, axis=-1)
    ids = (i1 * PEER_N_KEYS + i2).reshape(T, PEER_HEADS * PEER_TOPK)
    gates = jax.nn.softmax(fv, axis=-1).reshape(T, PEER_HEADS * PEER_TOPK)
    nblk = T // PEER_TOKEN_BLOCK

    def expert_block(args):
        tb, idb, gb = args
        u = jnp.take(u_tab, idb, axis=0)
        a = jax.nn.gelu(jnp.einsum('td,ted->te', tb, u).astype(jnp.float32), approximate=False)
        vv = jnp.take(v_tab, idb, axis=0)
        return jnp.einsum('te,ted->td', (gb * a).astype(vv.dtype), vv)

    out = lax.map(expert_block, (t.reshape(nblk, PEER_TOKEN_BLOCK, D),
                                 ids.reshape(nblk, PEER_TOKEN_BLOCK, -1),
                                 gates.reshape(nblk, PEER_TOKEN_BLOCK, -1)))
    return out.reshape(B, Lp, D).astype(h.dtype)

def setup_inputs(seed: int = 0) -> dict:
    key = jax.random.key(seed)
    ks = jax.random.split(key, 16)
    nrm = lambda k, shape: jax.random.normal(k, shape, jnp.float32)
    x = nrm(ks[0], (BATCH, SEQ, D_MODEL))
    meta_tokens = nrm(ks[1], (N_META, D_MODEL))
    ln_in_g = 1.0 + 0.02 * nrm(ks[2], (D_MODEL,))
    ln_in_b = 0.02 * nrm(ks[3], (D_MODEL,))
    beta = DEEPNORM_BETA
    col_scale = jnp.concatenate([
        jnp.ones((ATT_WIDTH + ATT_KV_WIDTH,), jnp.float32),
        jnp.full((ATT_KV_WIDTH,), beta, jnp.float32),
        jnp.ones((2 * RET_WIDTH,), jnp.float32),
        jnp.full((RET_WIDTH,), beta, jnp.float32),
        jnp.ones((RET_WIDTH,), jnp.float32)])
    w_in = nrm(ks[4], (DEPTH, D_MODEL, IN_COLS)) * (D_MODEL ** -0.5) * col_scale
    att_sinks = 0.5 * nrm(ks[5], (DEPTH, ATT_Q_HEADS))
    w_out = nrm(ks[6], (DEPTH, MIX_WIDTH, D_MODEL)) * (MIX_WIDTH ** -0.5) * beta
    ln_mix_g = 1.0 + 0.02 * nrm(ks[7], (DEPTH, D_MODEL))
    ln_mix_b = 0.02 * nrm(ks[8], (DEPTH, D_MODEL))
    peer_wq = nrm(ks[9], (DEPTH, D_MODEL, PEER_HEADS * PEER_D_KEY)) * (D_MODEL ** -0.5)
    peer_subkeys = nrm(ks[10], (DEPTH, PEER_HEADS, 2, PEER_N_KEYS, PEER_HALF)) * (PEER_HALF ** -0.5)
    peer_u = nrm(ks[11], (DEPTH, PEER_N_EXPERTS, D_MODEL)) * (D_MODEL ** -0.5)
    peer_v = nrm(ks[12], (DEPTH, PEER_N_EXPERTS, D_MODEL)) * beta
    ln_ffn_g = 1.0 + 0.02 * nrm(ks[13], (DEPTH, D_MODEL))
    ln_ffn_b = 0.02 * nrm(ks[14], (DEPTH, D_MODEL))
    return {"x": x, "meta_tokens": meta_tokens, "ln_in_g": ln_in_g, "ln_in_b": ln_in_b,
            "w_in": w_in, "att_sinks": att_sinks, "w_out": w_out,
            "ln_mix_g": ln_mix_g, "ln_mix_b": ln_mix_b,
            "peer_wq": peer_wq, "peer_subkeys": peer_subkeys, "peer_u": peer_u, "peer_v": peer_v,
            "ln_ffn_g": ln_ffn_g, "ln_ffn_b": ln_ffn_b}

def reference(x, meta_tokens, ln_in_g, ln_in_b, w_in, att_sinks, w_out, ln_mix_g, ln_mix_b,
              peer_wq, peer_subkeys, peer_u, peer_v, ln_ffn_g, ln_ffn_b):
    B = x.shape[0]
    pad = jnp.zeros((B, PAD, D_MODEL), x.dtype)
    meta = jnp.broadcast_to(meta_tokens.astype(x.dtype)[None], (B, N_META, D_MODEL))
    h = jnp.concatenate([pad, meta, x], axis=1)
    Lp = h.shape[1]
    slot = jnp.arange(Lp, dtype=jnp.int32)
    pos = slot - PAD
    key_valid = (slot >= PAD)[None, :, None].astype(x.dtype)
    h = layer_norm(h, ln_in_g, ln_in_b)
    for l in range(DEPTH):
        mix = hybrid_mixer(h, w_in[l], att_sinks[l], w_out[l], pos, key_valid)
        h = layer_norm(DEEPNORM_ALPHA * h + mix, ln_mix_g[l], ln_mix_b[l])
        ffn = peer(h, peer_wq[l], peer_subkeys[l], peer_u[l], peer_v[l])
        h = layer_norm(DEEPNORM_ALPHA * h + ffn, ln_ffn_g[l], ln_ffn_b[l])
    return h[:, BLOCK:]


_drawn_inputs = setup_inputs


def setup_inputs(seed=0):
    import zlib

    import numpy as np

    out = dict(_drawn_inputs(seed))
    spreads = {}
    factors = {'att_sinks': 8.0, 'ln_ffn_g': 2.779, 'ln_ffn_b': 2.788}
    for name, (base, spread) in spreads.items():
        noise = np.random.default_rng([zlib.crc32(name.encode()), seed]).standard_normal(out[name].shape)
        drawn = base * np.exp(spread * noise) if base else spread * noise
        out[name] = __import__('jax').numpy.asarray(drawn.astype(out[name].dtype))
    for name, factor in factors.items():
        out[name] = (out[name] * factor).astype(out[name].dtype)
    return out
```

```python
import math
from contextlib import ExitStack

import concourse.bass as bass
from concourse import mybir

F32 = mybir.dt.float32
U32 = mybir.dt.uint32
ALU = mybir.AluOpType
ACT = mybir.ActivationFunctionType
AX = mybir.AxisListType

P = 128
D = 2048
KC = D // P
META = 16
TILES = 2
TOK = TILES * P
KEYS = META + TOK
GCOLS = 512
HALF = KC // 2
NSLOT = 4
AQ_HEADS, AHD = 16, 64
RET_HEADS, RHD = 4, 256
COL_AK = AQ_HEADS * AHD
COL_RET = COL_AK + 4 * AHD
LN_EPS = 1e-5
ALPHA = 2.0 ** 0.25
NEG = -1e30
PH, TOPK, NKEY = 8, 16, 128
PICKS = PH * TOPK
OCT = 8
STEPS = PICKS // OCT
PARTS = 4

C_ROPE_A = 0
C_ROPE_R = C_ROPE_A + 3 * 64
C_MASK = C_ROPE_R + 3 * 256
C_DECAY = C_MASK + 144 + 256
C_END = C_DECAY + RET_HEADS * 2 * TOK


def projection_groups():
    groups = [("aq", 0, 512, (0, 1)), ("aq", 512, 512, (0, 1)), ("akv", COL_AK, 256, (0, 1, 2))]
    width = RET_HEADS * RHD
    for pair in range(2):
        for n, kind in enumerate(("rq", "rk", "rv", "rg")):
            groups.append((kind, COL_RET + n * width + pair * 512, 512,
                           (0, 1) if kind in ("rq", "rg") else (0, 1, 2)))
    return groups


GROUPS = projection_groups()


def schedule():
    rope = lambda g: [("rope", g, b) for b in GROUPS[g][3]]
    copy = lambda g: [("copy", g, b) for b in GROUPS[g][3]]
    att = [(g, t) for g in range(2) for t in range(TILES)]
    s = [("lnT", 0), ("lnT", 1), ("lnT", 2)]
    s += [("proj", 0), ("proj", 1)] + rope(0) + [("proj", 2)] + rope(1)
    s += [("proj", 3)] + rope(2) + [("proj", 4)] + rope(3) + [("attS", *att[0])]
    s += [("proj", 5)] + rope(4) + [("attO", *att[0]), ("attS", *att[1])]
    s += [("proj", 6)] + copy(5) + [("attO", *att[1]), ("attS", *att[2])]
    s += [("proj", 7)] + copy(6) + [("retS", 0)] + [("attO", *att[2]), ("attS", *att[3])] + [("retO", 0), ("retS", 1)]
    s += [("proj", 8)] + rope(7) + [("retT", 0), ("retO", 1), ("attO", *att[3])]
    s += [("proj", 9)] + rope(8) + [("retT", 1)]
    s += [("proj", 10)] + copy(9) + copy(10)
    s += [("retS", 2), ("retO", 2), ("retS", 3), ("retT", 2), ("retO", 3), ("retT", 3)]
    s += [("out", g) for g in range(4)] + [("subT", q) for q in range(4)]
    s += [("lnT", 3), ("lnT", 4)]
    s += [("pq", g) for g in range(4)] + [("ps", 0), ("ps", 1)]
    return s


SCHED = schedule()


class Plan:

    def __init__(self):
        self.unit = {}
        self.readers = []
        self.t = {}
        self.d = {}
        self.stage = {}
        self.stage_t = []
        counts = {"dve": 0, "act": 0}
        nt = nd = 0

        def tile(key, engines):
            self.unit[key] = len(self.readers)
            self.readers.append(tuple(engines))

        for job in SCHED:
            kind = job[0]
            if kind == "proj":
                g = job[1]
                who = {"aq": ("dve",), "akv": ("dve", "act"), "rq": ("dve",), "rk": ("dve",),
                       "rv": ("act",), "rg": ("act",)}[GROUPS[g][0]]
                for b in GROUPS[g][3]:
                    tile(("proj", g, b), who)
            elif kind == "out":
                for b in range(TILES):
                    tile(("out", job[1], b), ("dve",))
            elif kind == "pq":
                for b in range(2):
                    tile(("pq", job[1], b), ("act",))
            elif kind == "ps":
                for b in range(4):
                    tile(("ps", job[1], b), ("act",))
            n_t = {"lnT": 1 if job[1] == 2 else 4, "rope": 1, "attO": 4, "retT": 1, "subT": 1}.get(kind, 0)
            self.t[job] = list(range(nt, nt + n_t))
            nt += n_t
            n_d = {"attS": 4, "attO": 1, "retS": 2, "retO": 1}.get(kind, 0)
            self.d[job] = list(range(nd, nd + n_d))
            nd += n_d
            if kind == "rope":
                self.stage[job] = len(self.stage_t)
                self.stage_t.append(self.t[job][0])
        self.freed = []
        for who in self.readers:
            now = {}
            for e in who:
                counts[e] += 1
                now[e] = counts[e]
            self.freed.append(now)


PLAN = Plan()


def build(nc, x, meta, ln_in_g, ln_in_b, w_in, sinks, w_out, ln_mix_g, ln_mix_b, wq, subkeys,
          peer_u, peer_v, ln_ffn_g, ln_ffn_b, consts, ident_c, iota_c, out):
    with ExitStack() as ctx, ExitStack() as front:
        sem = lambda name: ctx.enter_context(nc.semaphore(name))
        keep = lambda name, shape, dt=F32: ctx.enter_context(nc.sbuf_tensor(name, shape, dt))
        sb = lambda name, shape, dt=F32: front.enter_context(nc.sbuf_tensor(name, shape, dt))

        ident = keep("ident", [P, P])
        iota16 = keep("iota16", [P, TOPK])
        h = keep("h", [P, TILES, D])
        gb = keep("gb", [P, 2, D])
        stats = keep("stats", [P, 4, 6])
        mv = keep("mv", [P, 2])
        rstd = keep("rstd", [P, 2])
        ids = keep("ids", [P, TILES, PICKS], U32)
        gates = keep("gates", [P, TILES, PICKS])
        hT = keep("hT", [P, KC, KEYS])
        work = keep("work", [P, 8 * TOK])
        qT = keep("qT", [P, 8, TOK])
        sc2 = keep("sc2", [P, P])

        consts_sb = sb("consts_sb", [P, C_END])
        w = sb("w", [P, NSLOT, HALF, GCOLS])
        mixT = sb("mixT", [P, KC, TOK])
        xm = mixT[0:META, 0:8, :].rearrange("p a b -> p (a b)")
        sink = sb("sink", [P, AQ_HEADS])
        ropeA = sb("ropeA", [P, GCOLS])
        ropeB = sb("ropeB", [P, GCOLS])
        stage = sb("stage", [P, 2, GCOLS])
        kT = sb("kT", [P, 2, KEYS])
        av = sb("av", [P, 3, P])
        rqT = sb("rqT", [P, 4, TOK])
        rkT = sb("rkT", [P, 4, KEYS])
        rvg = sb("rvg", [P, 5, GCOLS])
        rv, rg = rvg[:, 0:3, :], rvg[:, 3:5, :]
        skT = rvg[:, 0:4, :].rearrange("p a b -> p (a b)").rearrange("p (m n) -> p m n", m=16)
        prob = work[:, :].rearrange("p (h k) -> p h k", h=8)
        pT = sb("pT", [P, 2, 4, P])
        mx = sb("mx", [P, 4, 8])
        sT = sb("sT", [P, 5 * P])
        gated = sb("gated", [P, TILES, RHD])
        gn = sb("gn", [P, 2, TILES])

        def psum(name, dt=F32):
            return ctx.enter_context(nc.psum_tensor(name, [P, 512], dt))

        pj = [psum(f"pj{i}") for i in range(4)]
        tb = [psum(f"tb{i}") for i in range(2)]
        db = [psum(f"db{i}") for i in range(2)]

        consts_in = sem("consts_in")
        x_in = [sem(f"x_in{i}") for i in range(3)]
        gb_in = sem("gb_in")
        w_in_s = [sem(f"w_in{i}") for i in range(NSLOT)]
        w_used = sem("w_used")
        pj_full = sem("pj_full")
        pj_read = {"dve": sem("pj_read_dve"), "act": sem("pj_read_act")}
        t_full, t_read = sem("t_full"), sem("t_read")
        d_full, d_read = sem("d_full"), sem("d_read")
        stage_full = sem("stage_full")
        dve_step = sem("dve_step")
        act_step = sem("act_step")
        norm_var, norm_sd = sem("norm_var"), sem("norm_sd")
        ln_done = sem("ln_done")
        soft_max, soft_exp, soft_prob = sem("soft_max"), sem("soft_exp"), sem("soft_prob")
        ret_gated = sem("ret_gated")
        gate_ready, keys_taken = sem("gate_ready"), sem("keys_taken")
        sub_in, gvar, gsd = sem("sub_in"), sem("gvar"), sem("gsd")
        picks_ready = sem("picks_ready")
        fexp_in, fexp_out = sem("fexp_in"), sem("fexp_out")

        def rope_tab(kind, b, n):
            half = AHD // 2 if kind[0] == "a" else RHD // 2
            o = (C_ROPE_A if kind[0] == "a" else C_ROPE_R) + b * 2 * half
            return consts_sb[0:n, o:o + half], consts_sb[0:n, o + half:o + 2 * half]

        mask = [consts_sb[:, C_MASK:C_MASK + 144], consts_sb[:, C_MASK + 144:C_MASK + 400]]
        decay = consts_sb[:, C_DECAY:C_END].rearrange("p (h m q) -> p h m q", h=RET_HEADS, m=2)
        rows = lambda b: META if b == 2 else P
        spots = {0: (0, P), 1: (P, TOK), 2: (TOK, KEYS)}
        keyspots = {2: (0, META), 0: (META, META + P), 1: (META + P, KEYS)}
        lo = [0, META]
        nkeys = [META + P, TOK]
        pqT = mixT

        halves = []
        for _, c0, n, _ in GROUPS:
            halves += [(w_in, c0, n, 0), (w_in, c0, n, 1)]
        for src in (w_out, wq):
            for g in range(4):
                halves += [(src, g * 512, 512, 0), (src, g * 512, 512, 1)]
        subn = sb("subn", [P, 4, P])
        first_wq = 2 * (len(GROUPS) + 4)
        last_unit = [PLAN.unit[("proj", g, GROUPS[g][3][-1])] for g in range(len(GROUPS))]
        last_unit += [PLAN.unit[(kind, g, 1)] for kind in ("out", "pq") for g in range(4)]
        sub_in_q = [sem(f"sub_in{i}") for i in range(4)]

        front.close()
        U = keep("U", [P, OCT, D])
        V = keep("V", [P, OCT, D])
        idq = keep("idq", [P, 2, OCT], U32)
        dot = keep("dot", [P, OCT])
        ga = keep("ga", [P, OCT])
        wg = keep("wg", [P, OCT])
        diag = keep("diag", [P, OCT, P])
        alphaI = keep("alphaI", [P, P])
        u_in = [sem(f"u_in{i}") for i in range(OCT)]
        v_in = [sem(f"v_in{i}") for i in range(OCT)]
        u_free, v_free = sem("u_free"), sem("v_free")
        ids_staged = sem("ids_staged")
        slot_seen = sem("slot_seen")
        dots, gelus, weights, diags = sem("dots"), sem("gelus"), sem("weights"), sem("diags")
        alpha_ready = sem("alpha_ready")
        out_done = sem("out_done")
        acc = [tb + db, pj]

        small = lambda n: qT[:, n, :].rearrange("p (m k) -> p m k", m=16)
        sv, si, sif = small(0), small(1).bitcast(U32), small(2)
        fv = qT[:, 3, 0:PICKS].rearrange("p (m k) -> p m k", m=8)
        fi = qT[:, 3, PICKS:].bitcast(U32).rearrange("p (m k) -> p m k", m=8)
        by_half = lambda n: qT[:, n, :].rearrange("p (s m k) -> p s m k", s=2, m=8)
        fab, fabf, ex = by_half(4).bitcast(U32), by_half(5), by_half(6)
        gsum = qT[:, 7, 0:16].rearrange("p (s m) -> p s m", s=2)
        flat = hT[:, :, :].rearrange("p a b -> p (a b)")
        cand = flat[:, 0:2048].rearrange("p (m a b) -> p m a b", m=8, a=16)
        eq = flat[:, 2048:4096].rearrange("p (m a b) -> p m a b", m=8, a=16)

        block = ctx.enter_context(nc.Block())

        @block.sync
        def _(sp):
            sp.dma_start(h[:, 0, :], x[0:P, :]).then_inc(x_in[0], 16)
            sp.dma_start(gb[:, 0, :], ln_in_g.partition_broadcast(P)).then_inc(gb_in, 16)
            sp.dma_start(gb[:, 1, :], ln_in_b.partition_broadcast(P)).then_inc(gb_in, 16)
            sp.dma_start(ident[:, :], ident_c).then_inc(consts_in, 16)
            sp.dma_start(h[:, 1, :], x[P:TOK, :]).then_inc(x_in[1], 16)
            sp.dma_start(xm, meta).then_inc(x_in[2], 16)
            sp.dma_start(consts_sb[:, :], consts).then_inc(consts_in, 16)
            sp.dma_start(iota16[:, :], iota_c).then_inc(consts_in, 16)
            sp.dma_start(sink[:, :], sinks.partition_broadcast(P)).then_inc(consts_in, 16)
            for n, (src, c0, cols, half) in enumerate(halves):
                if n >= NSLOT:
                    group, second = divmod(n - NSLOT, 2)
                    if second or group >= len(GROUPS) + 4:
                        sp.wait_ge(pj_full, last_unit[group] + 1)
                    else:
                        sp.wait_ge(w_used, group + 1)
                sp.dma_start(w[:, n % NSLOT, :, 0:cols],
                             src[half * HALF * P:(half + 1) * HALF * P, c0:c0 + cols]
                             .rearrange("(k p) c -> p k c", p=P)).then_inc(w_in_s[n % NSLOT], 16)
                if n == 6:
                    sp.wait_ge(ln_done, 3)
                    sp.dma_start(gb[:, 0, :], ln_mix_g.partition_broadcast(P)).then_inc(gb_in, 16)
                    sp.dma_start(gb[:, 1, :], ln_mix_b.partition_broadcast(P)).then_inc(gb_in, 16)
                for q in {first_wq: (0,), first_wq + NSLOT - 1: (1, 2, 3)}.get(n, ()):
                    if q:
                        sp.wait_ge(t_full, PLAN.t[("subT", q - 1)][0] + 1)
                    sp.dma_start(subn[:, :, :], subkeys[:, 4 * q:4 * q + 4, :]).then_inc(sub_in_q[q], 16)
            sp.wait_ge(ln_done, 5)
            sp.dma_start(gb[:, 0, :], ln_ffn_g.partition_broadcast(P)).then_inc(gb_in, 16)
            sp.dma_start(gb[:, 1, :], ln_ffn_b.partition_broadcast(P)).then_inc(gb_in, 16)

            for tile in range(TILES):
                sp.wait_ge(ln_done, 6 + tile)
                sp.dma_start(out[tile * P:(tile + 1) * P, :], h[:, tile, :]).then_inc(out_done, 16)
            sp.wait_ge(out_done, 32)

        @block.tensor
        def _(pe):
            half_n = [0]

            def unit_bank(u):
                if u >= 4:
                    for e, n in PLAN.freed[u - 4].items():
                        pe.wait_ge(pj_read[e], n)
                return pj[u % 4]

            def t_bank(t):
                if t >= 2:
                    pe.wait_ge(t_read, t - 1)
                return tb[t % 2]

            def d_bank(d):
                if d >= 2:
                    pe.wait_ge(d_read, d - 1)
                return db[d % 2]

            def product(units, lhs, rows_of, cols):
                banks = {}
                for half in range(2):
                    n = half_n[0]
                    half_n[0] += 1
                    pe.wait_ge(w_in_s[n % NSLOT], 16 * (n // NSLOT + 1))
                    for b, u in units:
                        if half == 0:
                            banks[b] = unit_bank(u)
                        for k in range(HALF):
                            kk = half * HALF + k
                            last = nc.tensor.matmul(banks[b][0:rows_of(b), 0:cols], lhs(b, kk),
                                                    w[:, n % NSLOT, k, 0:cols], start=kk == 0, stop=kk == KC - 1)
                        if half == 1:
                            last.then_inc(pj_full, 1)
                    if half == 0:
                        last.then_inc(w_used, 1)

            for job in SCHED:
                kind = job[0]
                if kind == "lnT":
                    b = job[1] if job[1] < 3 else job[1] - 3
                    if job[1] == 0:
                        pe.wait_ge(consts_in, 64)
                    pe.wait_ge(ln_done, job[1] + 1)
                    if b == 2:
                        bank = t_bank(PLAN.t[job][0])
                        for k in range(KC):
                            last = nc.tensor.matmul(bank[:, k * META:(k + 1) * META], xm[:, k * P:(k + 1) * P],
                                                    ident[0:META, 0:META], start=True, stop=True)
                        last.then_inc(t_full, 1)
                    else:
                        for q, t in enumerate(PLAN.t[job]):
                            bank = t_bank(t)
                            for k in range(4):
                                kk = 4 * q + k
                                last = nc.tensor.transpose(bank[:, k * P:(k + 1) * P],
                                                           h[:, b, kk * P:(kk + 1) * P], ident[:, :])
                            last.then_inc(t_full, 1)
                elif kind == "proj":
                    g = job[1]
                    if g == 0:
                        pe.wait_ge(t_read, PLAN.t[("lnT", 2)][0] + 1)
                    cols = GROUPS[g][2]
                    product([(b, PLAN.unit[("proj", g, b)]) for b in GROUPS[g][3]],
                            lambda b, kk: hT[:, kk, spots[b][0]:spots[b][1]], rows, cols)
                elif kind == "rope":
                    _, g, b = job
                    t = PLAN.t[job][0]
                    pe.wait_ge(stage_full, PLAN.stage[job] + 1)
                    bank = t_bank(t)
                    src = stage[:, PLAN.stage[job] % 2, :]
                    n = rows(b)
                    for c in range(2 if g == 2 else 4):
                        if b == 2:
                            last = nc.tensor.matmul(bank[:, c * META:(c + 1) * META], src[0:META, c * P:(c + 1) * P],
                                                    ident[0:META, 0:META], start=True, stop=True)
                        else:
                            last = nc.tensor.transpose(bank[:, c * P:(c + 1) * P], src[:, c * P:(c + 1) * P], ident[:, :])
                    last.then_inc(t_full, 1)
                elif kind == "attS":
                    _, g, tile = job
                    if (g, tile) == (0, 0):
                        pe.wait_ge(t_read, PLAN.t[("rope", 2, 2)][0] + 1)
                    for i, d in enumerate(PLAN.d[job]):
                        bank = d_bank(d)
                        e = i % 2
                        for j in range(2):
                            last = nc.tensor.matmul(bank[:, j * nkeys[tile]:(j + 1) * nkeys[tile]],
                                                    qT[64 * e:64 * e + 64, 4 * g + 2 * (i // 2) + j, tile * P:(tile + 1) * P],
                                                    kT[64 * e:64 * e + 64, g, lo[tile]:lo[tile] + nkeys[tile]],
                                                    start=True, stop=True)
                        last.then_inc(d_full, 1)
                elif kind == "attO":
                    _, g, tile = job
                    n = 2 * g + tile
                    pe.wait_ge(soft_prob, n + 1)
                    n0 = META if tile == 0 else P
                    out_bank = None

                    def pv(pair):
                        pe.wait_ge(t_read, PLAN.t[job][pair] + 1)
                        for e in range(2):
                            o = out_bank[64 * e:64 * e + 64, pair * P:(pair + 1) * P]
                            nc.tensor.matmul(o, av[0:n0, 2 if tile == 0 else 0, 64 * g:64 * g + 64],
                                             pT[0:n0, pair % 2, 2 * e, :], start=True, stop=False)
                            last = nc.tensor.matmul(o, av[:, tile, 64 * g:64 * g + 64],
                                                    pT[:, pair % 2, 2 * e + 1, :], start=False, stop=True)
                        return last

                    for pair, t in enumerate(PLAN.t[job]):
                        bank = t_bank(t)
                        for e in range(2):
                            src = prob[:, 2 * pair + e, :]
                            if tile == 0:
                                nc.tensor.matmul(bank[0:META, 2 * e * P:(2 * e + 1) * P], src[:, 0:META], ident[:, :],
                                                 start=True, stop=True)
                            else:
                                nc.tensor.transpose(bank[:, 2 * e * P:(2 * e + 1) * P], src[:, 0:P], ident[:, :])
                            last = nc.tensor.transpose(bank[:, (2 * e + 1) * P:(2 * e + 2) * P], src[:, n0:n0 + P], ident[:, :])
                        last.then_inc(t_full, 1)
                        if pair == 1:
                            out_bank = d_bank(PLAN.d[job][0])
                        if pair >= 1:
                            pv(pair - 1)
                    pv(3).then_inc(d_full, 1)
                elif kind == "retS":
                    hd = job[1]
                    c = 2 * (hd % 2)
                    d0, d1 = PLAN.d[job]
                    pe.wait_ge(t_read, PLAN.t[("rope", 4 if hd < 2 else 8, 2)][0] + 1)
                    bank = d_bank(d0)
                    for k in range(2):
                        nc.tensor.matmul(bank[:, 0:TOK], rkT[:, c + k, META:META + P], rqT[:, c + k, :],
                                         start=k == 0, stop=k == 1)
                    for k in range(2):
                        last = nc.tensor.matmul(bank[:, TOK:TOK + P], rkT[:, c + k, META + P:KEYS], rqT[:, c + k, P:TOK],
                                                start=k == 0, stop=k == 1)
                    last.then_inc(d_full, 1)
                    bank = d_bank(d1)
                    for k in range(2):
                        last = nc.tensor.matmul(bank[0:META, 0:TOK], rkT[:, c + k, 0:META], rqT[:, c + k, :],
                                                start=k == 0, stop=k == 1)
                    last.then_inc(d_full, 1)
                elif kind == "retO":
                    hd = job[1]
                    pe.wait_ge(d_read, PLAN.d[("retS", hd)][1] + 1)
                    pe.wait_ge(pj_read["act"], PLAN.freed[PLAN.unit[("proj", 5 if hd < 2 else 9, 2)]]["act"])
                    bank = d_bank(PLAN.d[job][0])
                    v = lambda b: rv[0:rows(b), b, (hd % 2) * RHD:(hd % 2 + 1) * RHD]
                    nc.tensor.matmul(bank[:, 0:RHD], sT[0:META, 3 * P:4 * P], v(2), start=True, stop=False)
                    nc.tensor.matmul(bank[:, 0:RHD], sT[:, 0:P], v(0), start=False, stop=True)
                    nc.tensor.matmul(bank[:, RHD:2 * RHD], sT[0:META, 4 * P:5 * P], v(2), start=True, stop=False)
                    nc.tensor.matmul(bank[:, RHD:2 * RHD], sT[:, P:2 * P], v(0), start=False, stop=False)
                    nc.tensor.matmul(bank[:, RHD:2 * RHD], sT[:, 2 * P:3 * P], v(1), start=False,
                                     stop=True).then_inc(d_full, 1)
                elif kind == "retT":
                    hd = job[1]
                    pe.wait_ge(ret_gated, hd + 1)
                    bank = t_bank(PLAN.t[job][0])
                    for tile in range(TILES):
                        for c in range(2):
                            i = 2 * tile + c
                            last = nc.tensor.transpose(bank[:, i * P:(i + 1) * P], gated[:, tile, c * P:(c + 1) * P], ident[:, :])
                    last.then_inc(t_full, 1)
                elif kind == "subT":
                    q = job[1]
                    pe.wait_ge(sub_in_q[q], 16)
                    bank = t_bank(PLAN.t[job][0])
                    for c in range(4):
                        last = nc.tensor.transpose(bank[:, c * P:(c + 1) * P], subn[:, c, :], ident[:, :])
                    last.then_inc(t_full, 1)
                elif kind == "out":
                    if job[1] == 0:
                        pe.wait_ge(t_read, PLAN.t[("retT", 3)][0] + 1)
                        pe.wait_ge(d_read, PLAN.d[("attO", 1, 1)][0] + 1)
                    product([(b, PLAN.unit[("out", job[1], b)]) for b in range(TILES)],
                            lambda b, kk: mixT[:, kk, b * P:(b + 1) * P], rows, GCOLS)
                elif kind == "pq":
                    g = job[1]
                    if g == 0:
                        pe.wait_ge(t_read, PLAN.t[("lnT", 4)][3] + 1)
                    n0 = half_n[0]
                    half_n[0] += 2
                    for half in range(2):
                        pe.wait_ge(w_in_s[(n0 + half) % NSLOT], 16 * ((n0 + half) // NSLOT + 1))
                    for b in range(2):
                        u = PLAN.unit[("pq", g, b)]
                        bank = unit_bank(u)
                        for c in range(2):
                            for kk in range(KC):
                                last = nc.tensor.matmul(bank[:, c * TOK:(c + 1) * TOK],
                                                        w[:, (n0 + kk // HALF) % NSLOT, kk % HALF, (2 * b + c) * P:(2 * b + c + 1) * P],
                                                        hT[:, kk, 0:TOK], start=kk == 0, stop=kk == KC - 1)
                        last.then_inc(pj_full, 1)
                elif kind == "ps":
                    tile = job[1]
                    if tile == 0:
                        pe.wait_ge(pj_read["act"], PLAN.freed[PLAN.unit[("pq", 3, 1)]]["act"])
                        pe.wait_ge(t_read, PLAN.t[("subT", 3)][0] + 1)
                    for b in range(4):
                        bank = unit_bank(PLAN.unit[("ps", tile, b)])
                        for c in range(4):
                            m = 4 * b + c
                            last = nc.tensor.matmul(bank[:, c * P:(c + 1) * P], pqT[:, m, tile * P:(tile + 1) * P],
                                                    skT[:, m, :], start=True, stop=True)
                        last.then_inc(pj_full, 1)

            pe.wait_ge(alpha_ready, 1)
            pe.wait_ge(t_read, sum(map(len, PLAN.t.values())))
            pe.wait_ge(d_read, sum(map(len, PLAN.d.values())))
            for tile in range(TILES):
                if tile == 1:
                    pe.wait_ge(pj_read["act"], PLAN.freed[-1]["act"])
                for c in range(4):
                    nc.tensor.matmul(acc[tile][c][:, :], alphaI[:, :], h[:, tile, c * 512:(c + 1) * 512],
                                     start=True, stop=False, skip_group_check=True)
                with pe.Fori(0, STEPS) as i:
                    n = i + tile * STEPS
                    pe.wait_ge(diags, n + 1)
                    for k in range(OCT):
                        pe.wait_ge(v_in[k], (n + 1) * 16)
                        for c in range(4):
                            last = nc.tensor.matmul(acc[tile][c][:, :], diag[:, k, :], V[:, k, c * 512:(c + 1) * 512],
                                                    start=False, stop=False, skip_group_check=True)
                        last.then_inc(v_free, 1)

        @block.scalar
        def _(act):
            steps = [0]

            def link(ins):
                steps[0] += 1
                ins.then_inc(act_step, 1)
                act.wait_ge(act_step, steps[0])

            def norm_sqrt(n):
                act.wait_ge(norm_var, n + 1)
                nc.scalar.activation(rstd[:, 0:1], rstd[:, 0:1], ACT.Sqrt).then_inc(norm_sd, 1)

            def gate_exp(tile, part):
                act.wait_ge(fexp_in, tile * PARTS + part + 1)
                quarter = gates[:, tile, part * PICKS // PARTS:(part + 1) * PICKS // PARTS]
                nc.scalar.activation(quarter, quarter, ACT.Exp).then_inc(fexp_out, 1)

            for job in SCHED:
                kind = job[0]
                if kind == "lnT":
                    b = job[1] if job[1] < 3 else job[1] - 3
                    norm_sqrt(job[1])
                    if job[1] == 3:
                        act.wait_ge(pj_full, PLAN.unit[("proj", 10, 1)] + 1)
                    for q, t in enumerate(PLAN.t[job]):
                        act.wait_ge(t_full, t + 1)
                        if b == 2:
                            dst, src = hT[:, :, TOK:KEYS], tb[t % 2][:, 0:KC * META].rearrange("p (k n) -> p k n", k=KC)
                        else:
                            dst = hT[:, 4 * q:4 * q + 4, spots[b][0]:spots[b][1]]
                            src = tb[t % 2][:, :].rearrange("p (k n) -> p k n", k=4)
                        nc.scalar.copy(dst, src).then_inc(t_read, 1)
                elif kind == "rope":
                    _, g, b = job
                    t = PLAN.t[job][0]
                    gk = GROUPS[g][0]
                    if gk == "rq" and g == 7 and b == 0:
                        act.wait_ge(d_full, PLAN.d[("retS", 1)][1] + 1)
                    if gk == "akv":
                        u = PLAN.unit[("proj", g, b)]
                        act.wait_ge(pj_read["dve"], PLAN.freed[u]["dve"])
                        nc.scalar.copy(av[0:rows(b), b, :], pj[u % 4][0:rows(b), P:2 * P]).then_inc(pj_read["act"], 1)
                    act.wait_ge(t_full, t + 1)
                    n = rows(b)
                    nch = 2 if gk == "akv" else 4
                    src = tb[t % 2][:, 0:nch * n].rearrange("p (c n) -> p c n", c=nch)
                    k0, k1 = keyspots[b]
                    dst = {"aq": lambda: qT[:, 4 * g:4 * g + 4, b * P:(b + 1) * P],
                           "akv": lambda: kT[:, :, k0:k1],
                           "rq": lambda: rqT[:, :, b * P:(b + 1) * P],
                           "rk": lambda: rkT[:, :, k0:k1]}[gk]()
                    nc.scalar.copy(dst, src).then_inc(t_read, 1)
                elif kind == "copy":
                    _, g, b = job
                    u = PLAN.unit[("proj", g, b)]
                    act.wait_ge(pj_full, u + 1)
                    if g == 9 and b == 0:
                        act.wait_ge(d_full, PLAN.d[("retO", 1)][0] + 1)
                    if g == 10 and b == 0:
                        act.wait_ge(ret_gated, 2)
                    n = rows(b)
                    if GROUPS[g][0] == "rv":
                        nc.scalar.copy(rv[0:n, b, :], pj[u % 4][0:n, :]).then_inc(pj_read["act"], 1)
                    else:
                        nc.scalar.activation(rg[:, b, :], pj[u % 4][:, :], ACT.Silu).then_inc(pj_read["act"], 1)
                elif kind == "attS":
                    _, g, tile = job
                    n = 2 * g + tile
                    act.wait_ge(soft_max, n + 1)
                    for e in range(8):
                        nc.scalar.activation(prob[:, e, 0:nkeys[tile]], prob[:, e, 0:nkeys[tile]], ACT.Exp,
                                             bias=mx[:, 0, e:e + 1], accum_out=mx[:, 2, e:e + 1])
                    nc.scalar.activation(mx[:, 1, :], mx[:, 1, :], ACT.Exp).then_inc(soft_exp, 1)
                elif kind == "attO":
                    _, g, tile = job
                    n0 = META if tile == 0 else P
                    for pair, t in enumerate(PLAN.t[job]):
                        act.wait_ge(t_full, t + 1)
                        src = tb[t % 2][:, :].rearrange("p (e k n) -> p e k n", e=2, k=2)
                        dst = pT[:, pair % 2, :, :].rearrange("p (e k) n -> p e k n", e=2)
                        if tile == 0:
                            nc.scalar.copy(dst[0:META, :, 0, :], src[0:META, :, 0, :])
                            nc.scalar.copy(dst[:, :, 1, :], src[:, :, 1, :]).then_inc(t_read, 1)
                        else:
                            nc.scalar.copy(dst, src).then_inc(t_read, 1)
                elif kind == "retO":
                    act.wait_ge(gvar, job[1] + 1)
                    nc.scalar.activation(gn[:, 1, :], gn[:, 1, :], ACT.Sqrt).then_inc(gsd, 1)
                elif kind == "retT":
                    hd = job[1]
                    t = PLAN.t[job][0]
                    act.wait_ge(t_full, t + 1)
                    c0 = 8 + 2 * hd
                    nc.scalar.copy(mixT[:, c0:c0 + 2, :].rearrange("p c (t n) -> p t c n", t=2),
                                   tb[t % 2][:, :].rearrange("p (t c n) -> p t c n", t=2, c=2)).then_inc(t_read, 1)
                elif kind == "subT":
                    t = PLAN.t[job][0]
                    act.wait_ge(t_full, t + 1)
                    nc.scalar.copy(skT[:, 4 * job[1]:4 * job[1] + 4, :],
                                   tb[t % 2][:, :].rearrange("p (c n) -> p c n", c=4)).then_inc(t_read, 1)
                elif kind == "pq":
                    for b in range(2):
                        u = PLAN.unit[("pq", job[1], b)]
                        act.wait_ge(pj_full, u + 1)
                        m = 4 * job[1] + 2 * b
                        nc.scalar.copy(pqT[:, m:m + 2, :],
                                       pj[u % 4][:, :].rearrange("p (c n) -> p c n", c=2)).then_inc(pj_read["act"], 1)
                elif kind == "ps":
                    tile = job[1]
                    if tile == 1:
                        for part in range(PARTS):
                            gate_exp(0, part)
                        act.wait_ge(keys_taken, PARTS)
                    for b in range(4):
                        u = PLAN.unit[("ps", tile, b)]
                        act.wait_ge(pj_full, u + 1)
                        nc.scalar.copy(work[:, b * 512:(b + 1) * 512], pj[u % 4][:, :]).then_inc(pj_read["act"], 1)

            for tile in range(TILES):
                for part in range(PARTS if tile == 0 else 1):
                    steps_here = STEPS // PARTS if tile == 0 else STEPS
                    with act.Fori(0, steps_here) as i:
                        n = i + tile * STEPS + part * steps_here
                        act.wait_ge(u_free, (n + 2) * OCT)
                        nc.scalar.activation(ga[:, :], dot[:, :], ACT.Gelu).then_inc(gelus, 1)
                    if tile == 0:
                        gate_exp(1, part)
                act.wait_ge(norm_var, 6 + tile)
                nc.scalar.activation(rstd[:, 0:1], rstd[:, 0:1], ACT.Sqrt).then_inc(norm_sd, 1)

        dve_steps = [0]

        def link(ins):
            dve_steps[0] += 1
            ins.then_inc(dve_step, 1)
            nc.vector.wait_ge(dve_step, dve_steps[0])

        def layer_norm(t, n, number):
            for c in range(4):
                last = nc.vector.bn_stats(stats[0:n, c, :], t[:, c * 512:(c + 1) * 512])
            link(last)
            link(nc.vector.bn_aggr(mv[0:n, :], stats[0:n, :, :].rearrange("p a b -> p (a b)")))
            if n < P:
                link(nc.vector.memset(rstd[:, 0:1], 1.0))
            nc.vector.tensor_scalar_add(rstd[0:n, 0:1], mv[0:n, 1:2], LN_EPS).then_inc(norm_var, 1)
            nc.vector.wait_ge(norm_sd, number + 1)
            link(nc.vector.reciprocal(rstd[0:n, 1:2], rstd[0:n, 0:1]))
            link(nc.vector.tensor_scalar(t, t, mv[0:n, 0:1], rstd[0:n, 1:2], ALU.subtract, ALU.mult))
            link(nc.vector.tensor_tensor(t, t, gb[0:n, 0, :], ALU.mult))
            nc.vector.tensor_tensor(t, t, gb[0:n, 1, :], ALU.add).then_inc(ln_done, 1)

        @block.vector
        def _(dve):
            def picks(tile, part):
                if part == 0:
                    dve.wait_ge(pj_read["act"], PLAN.freed[PLAN.unit[("ps", tile, 3)]]["act"])
                n = tile * PARTS + part
                s3 = work[:, :].rearrange("p (m n) -> p m n", m=16)
                m0, m1 = 4 * part, 4 * part + 4
                for m in range(m0, m1):
                    link(nc.vector.max(sv[:, m, 0:8], s3[:, m, :]))
                    nc.vector.max_index(si[:, m, 0:8], sv[:, m, 0:8], s3[:, m, :])
                    link(nc.vector.match_replace(sc2[:, :], sv[:, m, 0:8], s3[:, m, :], -3e38))
                    link(nc.vector.max(sv[:, m, 8:16], sc2[:, :]))
                    link(nc.vector.max_index(si[:, m, 8:16], sv[:, m, 8:16], sc2[:, :]))
                nc.vector.tensor_copy(sif[:, m0:m1, :], si[:, m0:m1, :]).then_inc(keys_taken, 1)
                dve.wait_ge(keys_taken, n + 1)
                h0, h1 = 2 * part, 2 * part + 2
                halves_of = lambda t: t[:, m0:m1, :].rearrange("p (m s) k -> p m s k", s=2)
                grid = [P, 2, 16, 16]
                svp, sifp = halves_of(sv), halves_of(sif)
                c, e = cand[:, h0:h1, :, :], eq[:, h0:h1, :, :]
                link(nc.vector.tensor_tensor(c, svp[:, :, 0, :].unsqueeze(3).to_broadcast(grid),
                                             svp[:, :, 1, :].unsqueeze(2).to_broadcast(grid), ALU.add))
                cflat, eflat = c.rearrange("p m a b -> p m (a b)"), e.rearrange("p m a b -> p m (a b)")
                for m in range(2):
                    best, where = fv[:, h0 + m, :], fi[:, h0 + m, :]
                    link(nc.vector.max(best[:, 0:8], cflat[:, m, :]))
                    nc.vector.max_index(where[:, 0:8], best[:, 0:8], cflat[:, m, :])
                    link(nc.vector.match_replace(eflat[:, m, :], best[:, 0:8], cflat[:, m, :], -3e38))
                    link(nc.vector.max(best[:, 8:16], eflat[:, m, :]))
                    link(nc.vector.max_index(where[:, 8:16], best[:, 8:16], eflat[:, m, :]))
                gv = gates[:, tile, :].rearrange("p (m k) -> p m k", m=8)[:, h0:h1, :]
                nc.vector.tensor_tensor(gv, fv[:, h0:h1, :], fv[:, h0:h1, 0:1].to_broadcast([P, 2, 16]),
                                        ALU.subtract).then_inc(fexp_in, 1)
                nc.vector.tensor_single_scalar(fab[:, 0, h0:h1, :], fi[:, h0:h1, :], 4, ALU.logical_shift_right)
                link(nc.vector.tensor_single_scalar(fab[:, 1, h0:h1, :], fi[:, h0:h1, :], 15, ALU.bitwise_and))
                link(nc.vector.tensor_copy(fabf[:, :, h0:h1, :], fab[:, :, h0:h1, :]))
                for s in range(2):
                    link(nc.vector.tensor_tensor(e, fabf[:, s, h0:h1, :].unsqueeze(3).to_broadcast(grid),
                                                 iota16[:, :].unsqueeze(1).unsqueeze(1).to_broadcast(grid),
                                                 ALU.is_equal))
                    link(nc.vector.tensor_tensor(e, e, sifp[:, :, s, :].unsqueeze(2).to_broadcast(grid), ALU.mult))
                    link(nc.vector.reduce_sum(ex[:, s, h0:h1, :], e, AX.X))
                link(nc.vector.scalar_tensor_tensor(
                    out=ids[:, tile, :].rearrange("p (m k) -> p m k", m=8)[:, h0:h1, :], in0=ex[:, 0, h0:h1, :],
                    scalar=float(NKEY), in1=ex[:, 1, h0:h1, :], op0=ALU.mult, op1=ALU.add))
                dve.wait_ge(fexp_out, n + 1)
                link(nc.vector.reduce_sum(gsum[:, 0, h0:h1], gv, AX.X))
                link(nc.vector.reciprocal(gsum[:, 1, h0:h1], gsum[:, 0, h0:h1]))
                nc.vector.tensor_tensor(gv, gv, gsum[:, 1, h0:h1].unsqueeze(2).to_broadcast([P, 2, 16]),
                                        ALU.mult).then_inc(picks_ready, 1)

            def rope(src, dst, heads, half, cos, sin, n, twice):
                r = lambda a: a[0:n, 0:heads * 2 * half].rearrange("p (a s c) -> p a s c", a=heads, s=2)
                bc = lambda tab: tab.unsqueeze(1).unsqueeze(1).to_broadcast([n, heads, 2, half])
                a, b = r(ropeA), r(ropeB)
                s4 = src.rearrange("p (a s c) -> p a s c", a=heads, s=2)
                nc.vector.tensor_tensor(a, s4, bc(cos), ALU.mult)
                ins = nc.vector.tensor_tensor(b, s4, bc(sin), ALU.mult)
                ins.then_inc(pj_read["dve"], 1)
                return a, b

            for job in SCHED:
                kind = job[0]
                if kind == "lnT":
                    j = job[1]
                    b = j if j < 3 else j - 3
                    if j < 3:
                        dve.wait_ge(x_in[b], 16)
                        if j == 0:
                            dve.wait_ge(gb_in, 32)
                    elif j == 3:
                        dve.wait_ge(gb_in, 64)
                    layer_norm(xm if b == 2 else h[:, b, :], rows(b), j)
                elif kind == "rope":
                    _, g, b = job
                    gk = GROUPS[g][0]
                    u = PLAN.unit[("proj", g, b)]
                    n = rows(b)
                    half = AHD // 2 if gk[0] == "a" else RHD // 2
                    heads = {"aq": 8, "akv": 2, "rq": 2, "rk": 2}[gk]
                    cos, sin = rope_tab(gk, b, n)
                    if g == 0 and b == 0:
                        dve.wait_ge(consts_in, 64)
                    dve.wait_ge(pj_full, u + 1)
                    a, bb = rope(pj[u % 4][0:n, 0:heads * 2 * half], None, heads, half, cos, sin, n, gk == "akv")
                    dve.wait_ge(pj_read["dve"], PLAN.freed[u]["dve"])
                    s = PLAN.stage[job]
                    if s >= 2:
                        dve.wait_ge(t_full, PLAN.stage_t[s - 2] + 1)
                    st = stage[0:n, s % 2, :]
                    if gk == "akv":
                        o = st[:, 0:2 * P].rearrange("p (a t s c) -> p a t s c", a=2, t=2, s=2)
                        for copy in range(2):
                            nc.vector.tensor_tensor(o[:, :, copy, 0, :], a[:, :, 0, :], bb[:, :, 1, :], ALU.subtract)
                            last = nc.vector.tensor_tensor(o[:, :, copy, 1, :], a[:, :, 1, :], bb[:, :, 0, :], ALU.add)
                    else:
                        o = st.rearrange("p (a s c) -> p a s c", a=heads, s=2)
                        nc.vector.tensor_tensor(o[:, :, 0, :], a[:, :, 0, :], bb[:, :, 1, :], ALU.subtract)
                        last = nc.vector.tensor_tensor(o[:, :, 1, :], a[:, :, 1, :], bb[:, :, 0, :], ALU.add)
                    last.then_inc(stage_full, 1)
                    dve.wait_ge(stage_full, s + 1)
                elif kind == "attS":
                    _, g, tile = job
                    n = 2 * g + tile
                    nk = nkeys[tile]
                    if n:
                        before = ("attO", (n - 1) // 2, (n - 1) % 2)
                        dve.wait_ge(t_full, PLAN.t[before][3] + 1)
                    for i, d in enumerate(PLAN.d[job]):
                        dve.wait_ge(d_full, d + 1)
                        h0 = 4 * (i // 2) + i % 2
                        nc.vector.scalar_tensor_tensor(
                            out=prob[:, h0:h0 + 3:2, 0:nk],
                            in0=db[d % 2][:, 0:2 * nk].rearrange("p (e k) -> p e k", e=2), scalar=AHD ** -0.5,
                            in1=mask[tile].unsqueeze(1).to_broadcast([P, 2, nk]),
                            op0=ALU.mult, op1=ALU.add).then_inc(d_read, 1)
                    dve.wait_ge(d_read, PLAN.d[job][3] + 1)
                    link(nc.vector.reduce_max(mx[:, 1, :], prob[:, :, 0:nk], AX.X))
                    sk = sink[:, 8 * g:8 * g + 8]
                    link(nc.vector.tensor_tensor(mx[:, 1, :], mx[:, 1, :], sk, ALU.max))
                    link(nc.vector.tensor_scalar_mul(mx[:, 0, :], mx[:, 1, :], -1.0))
                    nc.vector.tensor_tensor(mx[:, 1, :], sk, mx[:, 0, :], ALU.add).then_inc(soft_max, 1)
                    dve.wait_ge(soft_exp, n + 1)
                    link(nc.vector.tensor_tensor(mx[:, 2, :], mx[:, 2, :], mx[:, 1, :], ALU.add))
                    link(nc.vector.reciprocal(mx[:, 2, :], mx[:, 2, :]))
                    nc.vector.tensor_tensor(prob[:, :, 0:nk], prob[:, :, 0:nk],
                                            mx[:, 2, :].unsqueeze(2).to_broadcast([P, 8, nk]),
                                            ALU.mult).then_inc(soft_prob, 1)
                elif kind == "attO":
                    _, g, tile = job
                    d = PLAN.d[job][0]
                    dve.wait_ge(d_full, d + 1)
                    nc.vector.tensor_copy(mixT[:, 4 * g:4 * g + 4, tile * P:(tile + 1) * P],
                                          db[d % 2][:, :].rearrange("p (c n) -> p c n", c=4)).then_inc(d_read, 1)
                elif kind == "retS":
                    hd = job[1]
                    d0, d1 = PLAN.d[job]
                    if hd:
                        dve.wait_ge(d_full, PLAN.d[("retO", hd - 1)][0] + 1)
                    dve.wait_ge(d_full, d0 + 1)
                    nc.vector.tensor_tensor(sT[:, 0:TOK], db[d0 % 2][:, 0:TOK], decay[:, hd, 0, :], ALU.mult)
                    nc.vector.tensor_tensor(sT[:, TOK:TOK + P], db[d0 % 2][:, TOK:TOK + P], decay[:, hd, 0, 0:P],
                                            ALU.mult).then_inc(d_read, 1)
                    dve.wait_ge(d_full, d1 + 1)
                    nc.vector.tensor_tensor(sT[0:META, 3 * P:5 * P], db[d1 % 2][0:META, 0:TOK], decay[0:META, hd, 1, :],
                                            ALU.mult).then_inc(d_read, 1)
                elif kind == "retO":
                    hd = job[1]
                    d = PLAN.d[job][0]
                    dve.wait_ge(d_full, d + 1)
                    if hd:
                        dve.wait_ge(t_full, PLAN.t[("retT", hd - 1)][0] + 1)
                    bank = db[d % 2][:, :].rearrange("p (t e) -> p t e", t=2)
                    for tile in range(TILES):
                        link(nc.vector.bn_stats(stats[:, 0, :], bank[:, tile, :]))
                        link(nc.vector.bn_aggr(mv[:, :], stats[:, 0, :]))
                        link(nc.vector.tensor_copy(gn[:, 0, tile:tile + 1], mv[:, 0:1]))
                        last = nc.vector.tensor_scalar_add(gn[:, 1, tile:tile + 1], mv[:, 1:2], LN_EPS)
                        if tile == 0:
                            link(last)
                    last.then_inc(gvar, 1)
                    dve.wait_ge(gsd, hd + 1)
                    link(nc.vector.reciprocal(gn[:, 1, :], gn[:, 1, :]))
                    for tile in range(TILES):
                        last = nc.vector.tensor_scalar(gated[:, tile, :], bank[:, tile, :], gn[:, 0, tile:tile + 1],
                                                       gn[:, 1, tile:tile + 1], ALU.subtract, ALU.mult)
                    last.then_inc(d_read, 1)
                    dve.wait_ge(d_read, d + 1)
                    dve.wait_ge(pj_read["act"], PLAN.freed[PLAN.unit[("proj", 6 if hd < 2 else 10, 1)]]["act"])
                    nc.vector.tensor_tensor(gated[:, :, :], gated[:, :, :],
                                            rg[:, :, (hd % 2) * RHD:(hd % 2 + 1) * RHD], ALU.mult).then_inc(ret_gated, 1)
                elif kind == "out":
                    g = job[1]
                    for b in range(TILES):
                        u = PLAN.unit[("out", g, b)]
                        dve.wait_ge(pj_full, u + 1)
                        hs = h[:, b, g * 512:(g + 1) * 512]
                        nc.vector.scalar_tensor_tensor(out=hs, in0=hs, scalar=ALPHA, in1=pj[u % 4][:, :],
                                                       op0=ALU.mult, op1=ALU.add).then_inc(pj_read["dve"], 1)
                    if g == 3:
                        dve.wait_ge(pj_read["dve"], PLAN.freed[u]["dve"])
                elif kind == "ps" and job[1] == 0:
                    for part in range(PARTS):
                        picks(0, part)

            dve.wait_ge(pj_full, len(PLAN.freed))
            nc.vector.tensor_scalar_mul(alphaI[:, :], ident[:, :], ALPHA).then_inc(alpha_ready, 1)
            for tile in range(TILES):
                for part in range(PARTS if tile == 0 else 1):
                    steps_here = STEPS // PARTS if tile == 0 else STEPS
                    with dve.Fori(0, steps_here) as i:
                        step = i + part * steps_here
                        n = step + tile * STEPS
                        for k in range(OCT):
                            dve.wait_ge(u_in[k], (n + 1) * 16)
                            nc.vector.tensor_tensor_reduce(out=U[:, k, :], in0=U[:, k, :], in1=h[:, tile, :], scale=1.0,
                                                           scalar=0.0, op0=ALU.mult, op1=ALU.add,
                                                           accum_out=dot[:, k:k + 1]).then_inc(u_free, 1)
                        dve.wait_ge(gelus, n + 1)
                        nc.vector.tensor_tensor(wg[:, :], ga[:, :], gates[:, tile, bass.ts(step, OCT)],
                                                ALU.mult).then_inc(weights, 1)
                        dve.wait_ge(weights, n + 1)
                        dve.wait_ge(v_free, (n + 1) * OCT)
                        nc.vector.tensor_tensor(diag[:, :, :], ident[:, :].unsqueeze(1).to_broadcast([P, OCT, P]),
                                                wg[:, :].unsqueeze(2).to_broadcast([P, OCT, P]), ALU.mult).then_inc(diags, 1)
                    if tile == 0:
                        picks(1, part)
                dve.wait_ge(v_free, OCT * (1 + (tile + 1) * STEPS))
                for c in range(4):
                    last = nc.vector.tensor_copy(h[:, tile, c * 512:(c + 1) * 512], acc[tile][c][:, :])
                link(last)
                dve.wait_ge(gb_in, 96)
                layer_norm(h[:, tile, :], P, 5 + tile)

        @block.gpsimd
        def _(pool):
            pool.wait_ge(pj_full, len(PLAN.freed))
            nc.gpsimd.engine_nop().then_inc(u_free, OCT)
            nc.gpsimd.engine_nop().then_inc(v_free, OCT)
            for quarter in range(TILES * PARTS):
                tile, part = divmod(quarter, PARTS)
                pool.wait_ge(picks_ready, quarter + 1)
                with pool.Fori(0, STEPS // PARTS // 2) as i:
                    for turn in range(2):
                        step = i * 2 + turn + part * (STEPS // PARTS)
                        n = step + tile * STEPS
                        nc.gpsimd.tensor_copy(idq[:, turn, :], ids[:, tile, bass.ts(step, OCT)]).then_inc(ids_staged, 1)
                        pool.wait_ge(ids_staged, n + 1)
                        for table, slots, free, land in ((peer_u, U, u_free, u_in), (peer_v, V, v_free, v_in)):
                            for k in range(OCT):
                                pool.wait_ge(free, n * OCT + k + 1)
                                nc.gpsimd.sem_inc(slot_seen, 1)
                                nc.gpsimd.indirect_dma_start(
                                    out=slots[:, k, :], out_offset=None, in_=table,
                                    in_offset=bass.IndirectOffsetOnAxis(ap=idq[:, turn, k:k + 1], axis=0)
                                ).then_inc(land[k], 16)


def constants():
    import numpy as np
    f = np.float32
    c = np.zeros((P, C_END), f)
    for b, first in ((0, META), (1, META + P), (2, 0)):
        pos = (first + np.arange(P)).astype(f)
        for dh, o in ((AHD, C_ROPE_A), (RHD, C_ROPE_R)):
            inv = f(10000.0) ** (-np.arange(0, dh, 2, dtype=f) / f(dh))
            ang = (pos[:, None] * inv[None, :]).astype(f)
            w = dh // 2
            c[:, o + b * dh:o + b * dh + w] = np.cos(ang.astype(np.float64))
            c[:, o + b * dh + w:o + (b + 1) * dh] = np.sin(ang.astype(np.float64))
    i = np.arange(P)[:, None]
    for o, lo, keys, tile in ((C_MASK, 0, META + P, 0), (C_MASK + META + P, META, TOK, 1)):
        diff = (META + tile * P + i) - (lo + np.arange(keys)[None, :])
        c[:, o:o + keys] = np.where((diff >= 0) & (diff < 128), 0.0, NEG)
    q = np.arange(TOK)[None, :]
    for hd in range(RET_HEADS):
        g = 1.0 - 2.0 ** (-5.0 - hd)
        own = np.where(q - i >= 0, g ** np.maximum(q - i, 0).astype(np.float64), 0.0)
        met = g ** (q + META - i).astype(np.float64)
        o = C_DECAY + hd * 2 * TOK
        c[:, o:o + TOK] = own * RHD ** -0.5
        c[:, o + TOK:o + 2 * TOK] = met * RHD ** -0.5
    return c, np.eye(P, dtype=f), np.tile(np.arange(TOPK, dtype=f), (P, 1))


def kernel(x, meta_tokens, ln_in_g, ln_in_b, w_in, att_sinks, w_out, ln_mix_g, ln_mix_b,
           peer_wq, peer_subkeys, peer_u, peer_v, ln_ffn_g, ln_ffn_b):
    import numpy as np
    import concourse.bacc as bacc
    from concourse.bass_utils import run_bass_kernel_spmd

    nc = bacc.Bacc("TRN2", target_bir_lowering=False, num_devices=1)
    consts, ident, iota = constants()
    given = {
        "x": np.asarray(x)[0], "meta": meta_tokens, "ln_in_g": ln_in_g, "ln_in_b": ln_in_b,
        "w_in": np.asarray(w_in)[0], "sinks": np.asarray(att_sinks)[0], "w_out": np.asarray(w_out)[0],
        "ln_mix_g": np.asarray(ln_mix_g)[0], "ln_mix_b": np.asarray(ln_mix_b)[0],
        "wq": np.asarray(peer_wq)[0],
        "subkeys": np.asarray(peer_subkeys)[0].reshape(2 * PH, NKEY, P).transpose(1, 0, 2),
        "peer_u": np.asarray(peer_u)[0], "peer_v": np.asarray(peer_v)[0],
        "ln_ffn_g": np.asarray(ln_ffn_g)[0], "ln_ffn_b": np.asarray(ln_ffn_b)[0],
        "consts": consts, "ident_c": ident, "iota_c": iota,
    }
    arrays, args = {}, []
    for name, value in given.items():
        arrays["in_" + name] = a = np.ascontiguousarray(value)
        args.append(nc.dram_tensor("in_" + name, a.shape, mybir.dt.from_np(a.dtype), kind="ExternalInput").ap())
    out = nc.dram_tensor("layer_out", (TOK, D), F32, kind="ExternalOutput").ap()
    build(nc, *args, out)
    r = run_bass_kernel_spmd(nc, [arrays], core_ids=[0])
    return np.asarray(r.results[0]["layer_out"]).reshape(1, TOK, D)
```

```python
import math
from contextlib import ExitStack

import concourse.bass as bass
from concourse import mybir

F32 = mybir.dt.float32
F32R = mybir.dt.float32r
U32 = mybir.dt.uint32
ALU = mybir.AluOpType
ACT = mybir.ActivationFunctionType
AX = mybir.AxisListType

P = 128
D = 2048
KC = D // P
META = 16
TILES = 2
TOK = TILES * P
KEYS = META + TOK
GCOLS = 512
QK = 4
QUARTERS = KC // QK
NRAW, NSPLIT = 2, 3
AQ_HEADS, AHD = 16, 64
RET_HEADS, RHD = 4, 256
COL_AK = AQ_HEADS * AHD
COL_RET = COL_AK + 4 * AHD
LN_EPS = 1e-5
ALPHA = 2.0 ** 0.25
NEG = -1e30
PH, TOPK, NKEY = 8, 16, 128
PICKS = PH * TOPK
OCT = 8
STEPS = PICKS // OCT
PARTS = 4

C_ROPE_A = 0
C_ROPE_R = C_ROPE_A + 3 * 64
C_MASK = C_ROPE_R + 3 * 256
C_DECAY = C_MASK + 144 + 256
C_END = C_DECAY + RET_HEADS * 2 * TOK


def projection_groups():
    groups = [("aq", 0, 512, (0, 1)), ("aq", 512, 512, (0, 1)), ("akv", COL_AK, 256, (0, 1, 2))]
    width = RET_HEADS * RHD
    for pair in range(2):
        for n, kind in enumerate(("rq", "rk", "rv", "rg")):
            groups.append((kind, COL_RET + n * width + pair * 512, 512,
                           (0, 1) if kind in ("rq", "rg") else (0, 1, 2)))
    return groups


GROUPS = projection_groups()


def schedule():
    rope = lambda g: [("rope", g, b) for b in GROUPS[g][3]]
    copy = lambda g: [("copy", g, b) for b in GROUPS[g][3]]
    att = [(g, t) for g in range(2) for t in range(TILES)]
    s = [("lnT", 0), ("lnT", 1), ("lnT", 2)]
    s += [("proj", 0), ("proj", 1)] + rope(0) + [("proj", 2)] + rope(1) + copy(2)
    s += [("proj", 3)] + rope(2) + [("proj", 4)] + rope(3) + [("attS", *att[0])]
    s += [("proj", 5)] + rope(4) + [("attO", *att[0]), ("attS", *att[1])] + copy(5)
    s += [("proj", 6), ("attO", *att[1]), ("attS", *att[2])] + copy(6)
    s += [("proj", 7), ("retS", 0), ("attO", *att[2]), ("attS", *att[3]), ("retO", 0), ("retS", 1)]
    s += [("proj", 8)] + rope(7) + [("retT", 0), ("retO", 1), ("attO", *att[3])]
    s += [("proj", 9)] + rope(8) + [("retT", 1)] + copy(9) + [("retS", 2)]
    s += [("proj", 10)] + copy(10) + [("retO", 2), ("retS", 3)]
    s += [("out", 0, 0, 3), ("retT", 2), ("retO", 3), ("retT", 3), ("out", 0, 3, 4)]
    s += [("out", g, 0, 4) for g in (1, 2, 3)] + [("subT", q) for q in range(4)]
    s += [("lnT", 3), ("lnT", 4)]
    s += [("pq", g) for g in range(4)] + [("ps", 0), ("ps", 1)]
    return s


SCHED = schedule()


class Plan:

    def __init__(self):
        self.unit = {}
        self.readers = []
        self.t = {}
        self.d = {}
        self.stage = {}
        self.stage_t = []
        self.t_read = []
        counts = {"dve": 0, "act": 0}
        t_counts = {"dve": 0, "act": 0}
        self.t_split = {}
        nt = nd = 0

        def tile(key, engines):
            self.unit[key] = len(self.readers)
            self.readers.append(tuple(engines))

        for job in SCHED:
            kind = job[0]
            if kind == "proj":
                g = job[1]
                who = {"aq": ("dve",), "akv": ("dve", "act"), "rq": ("dve",), "rk": ("dve",),
                       "rv": ("act",), "rg": ("act",)}[GROUPS[g][0]]
                for b in GROUPS[g][3]:
                    tile(("proj", g, b), who)
            elif kind == "out" and job[2] == 0:
                for b in range(TILES):
                    tile(("out", job[1], b), ("dve",))
            elif kind == "pq":
                for b in range(4):
                    tile(("pq", job[1], b), ("act",))
            elif kind == "ps":
                for b in range(4):
                    tile(("ps", job[1], b), ("act",))
            n_t = {"lnT": 1 if job[1] == 2 else 4, "rope": 1, "attO": 4, "retT": 1, "subT": 1}.get(kind, 0)
            self.t[job] = list(range(nt, nt + n_t))
            nt += n_t
            for t in self.t[job]:
                last = "dve" if kind in ("lnT", "retT") else "act"
                if last == "dve":
                    self.t_split[t] = len(self.t_split)
                t_counts[last] += 1
                self.t_read.append((last, t_counts[last]))
            n_d = {"attS": 4, "attO": 1, "retS": 2, "retO": 1}.get(kind, 0)
            self.d[job] = list(range(nd, nd + n_d))
            nd += n_d
            if kind == "rope":
                self.stage[job] = len(self.stage_t)
                self.stage_t.append(self.t[job][0])
        self.freed = []
        for who in self.readers:
            now = {}
            for e in who:
                counts[e] += 1
                now[e] = counts[e]
            self.freed.append(now)


PLAN = Plan()


def build(nc, x, meta, ln_in_g, ln_in_b, w_in, sinks, w_out, ln_mix_g, ln_mix_b, wq, subkeys,
          peer_u, peer_v, ln_ffn_g, ln_ffn_b, consts, ident_c, iota_c, out):
    with ExitStack() as ctx:
        sem = lambda name: ctx.enter_context(nc.semaphore(name))

        def at(name, shape, offset, dt=F32):
            return nc.alloc_sbuf_tensor_at(name, [P] + shape, dt, offset=offset)

        small = lambda name, shape, dt=F32: ctx.enter_context(nc.sbuf_tensor(name, [P] + shape, dt))
        ident = small("ident", [P])
        iota16 = small("iota16", [TOPK])
        stats = small("stats", [TILES, 4, 6])
        mv = small("mv", [2])
        rstd = small("rstd", [2])
        ids = small("ids", [TILES, PICKS], U32)
        gates = small("gates", [TILES, PICKS])
        sc2 = small("sc2", [P])
        sink = small("sink", [AQ_HEADS])
        mx = small("mx", [4, 8])
        gn = small("gn", [2, TILES])
        dot, ga, wg = small("dot", [OCT]), small("ga", [OCT]), small("wg", [OCT])
        idq = small("idq", [2, OCT], U32)

        KB = 1024
        r_stream = -(-nc.sbuf_base // 32) * 32
        r_hT = r_stream + 4 * (4 * TOK + 4 * KEYS + 5 * GCOLS)
        r_work = r_hT + 4 * KC * KEYS
        r_qT = r_work + 8 * KB
        r_rest = r_qT + 8 * KB
        r_hT_lo = r_rest
        r_mix = r_hT_lo + 4 * KC * KEYS
        r_raw = r_mix + 32 * KB
        r_split = r_raw + NRAW * 8 * KB
        r_tab = r_split + NSPLIT * 16 * KB
        r_misc = r_tab + 4 * (C_END + 2 * GCOLS)

        h = at("h", [TILES, D], r_stream)
        rqT = at("rqT", [4, TOK], r_stream)
        rkT = at("rkT", [4, KEYS], r_stream + 16 * TOK)
        rvg = at("rvg", [5, GCOLS], r_stream + 16 * TOK + 16 * KEYS)
        rv, rg = rvg[:, 0:3, :], rvg[:, 3:5, :]

        hT = at("hT", [KC, KEYS], r_hT, F32R)
        hT_lo = at("hT_lo", [KC, KEYS], r_hT_lo, F32R)
        mixT = at("mixT", [KC, TOK], r_mix, F32R)
        mixT_lo = at("mixT_lo", [KC, TOK], r_mix + 16 * KB, F32R)
        w_raw = at("w_raw", [NRAW, QK, GCOLS], r_raw)
        w_hi = at("w_hi", [NSPLIT, QK, GCOLS], r_split, F32R)
        w_lo = at("w_lo", [NSPLIT, QK, GCOLS], r_split + NSPLIT * 8 * KB, F32R)

        gb = at("gb", [2, D], r_tab)
        consts_sb = at("consts_sb", [C_END], r_tab)
        ropeA = at("ropeA", [GCOLS], r_tab + 4 * C_END)
        ropeB = at("ropeB", [GCOLS], r_tab + 4 * (C_END + GCOLS))

        xm_t = at("xm", [D], r_mix)
        xm = xm_t[0:META, :]
        pqT = at("pqT", [2 * PH, TOK], r_mix)
        skT = at("skT", [2 * PH, NKEY], r_mix + 16 * KB)
        subn = at("subn", [4, P], r_mix + 24 * KB)

        work = at("work", [8 * TOK], r_work)
        prob = work[:, :].rearrange("p (h k) -> p h k", h=8)
        qT = at("qT", [8, TOK], r_qT)
        stage = at("stage", [2, GCOLS], r_misc)
        pT = at("pT", [2, 4, P], r_misc + 4 * KB)
        kT = at("kT", [2, KEYS], r_misc + 8 * KB)
        av = at("av", [3, P], r_misc + 8 * KB + 8 * KEYS)
        sT = at("sT", [5 * P], r_misc + 8 * KB + 8 * KEYS + 12 * P)
        gated = at("gated", [TILES, RHD], r_misc + 8 * KB + 8 * KEYS + 32 * P)

        U = at("U", [OCT, D], r_rest)
        V = at("V", [OCT, D], r_rest + 64 * KB)
        diag = at("diag", [OCT, P], r_rest + 128 * KB)
        gb_last = at("gb_last", [2, D], r_rest + 132 * KB)
        alphaI = at("alphaI", [P], r_rest + 148 * KB)
        h_saved = nc.dram_tensor("h_saved", (TOK, D), F32, kind="Internal").ap()

        def psum(name, dt=F32):
            return ctx.enter_context(nc.psum_tensor(name, [P, 512], dt))

        pj = [psum(f"pj{i}") for i in range(4)]
        tb = [psum(f"tb{i}") for i in range(2)]
        db = [psum(f"db{i}") for i in range(2)]

        consts_in = sem("consts_in")
        x_in = [sem(f"x_in{i}") for i in range(3)]
        gb_in = sem("gb_in")
        raw_in = [sem(f"raw_in{i}") for i in range(NRAW)]
        hi_done, lo_done = sem("hi_done"), sem("lo_done")
        w_used = sem("w_used")
        saved, back = sem("saved"), sem("back")
        tables_in = sem("tables_in")
        pj_full = sem("pj_full")
        pj_read = {"dve": sem("pj_read_dve"), "act": sem("pj_read_act")}
        t_full, t_hi = sem("t_full"), sem("t_hi")
        t_read = {"dve": sem("t_read_dve"), "act": sem("t_read_act")}
        d_full, d_read = sem("d_full"), sem("d_read")
        stage_full = sem("stage_full")
        dve_step = sem("dve_step")
        act_step = sem("act_step")
        norm_var, norm_sd = sem("norm_var"), sem("norm_sd")
        ln_done = sem("ln_done")
        soft_max, soft_exp, soft_prob = sem("soft_max"), sem("soft_exp"), sem("soft_prob")
        ret_gated = sem("ret_gated")
        gate_ready, keys_taken = sem("gate_ready"), sem("keys_taken")
        sub_in, gvar, gsd = sem("sub_in"), sem("gvar"), sem("gsd")
        picks_ready = sem("picks_ready")
        fexp_in, fexp_out = sem("fexp_in"), sem("fexp_out")

        def rope_tab(kind, b, n):
            half = AHD // 2 if kind[0] == "a" else RHD // 2
            o = (C_ROPE_A if kind[0] == "a" else C_ROPE_R) + b * 2 * half
            return consts_sb[0:n, o:o + half], consts_sb[0:n, o + half:o + 2 * half]

        mask = [consts_sb[:, C_MASK:C_MASK + 144], consts_sb[:, C_MASK + 144:C_MASK + 400]]
        decay = consts_sb[:, C_DECAY:C_END].rearrange("p (h m q) -> p h m q", h=RET_HEADS, m=2)
        rows = lambda b: META if b == 2 else P
        spots = {0: (0, P), 1: (P, TOK), 2: (TOK, KEYS)}
        keyspots = {2: (0, META), 0: (META, META + P), 1: (META + P, KEYS)}
        lo = [0, META]
        nkeys = [META + P, TOK]
        loads = [(w_in, c0, n, q) for _, c0, n, _ in GROUPS for q in range(QUARTERS)]
        loads += [(src, g * GCOLS, GCOLS, q) for src in (w_out, wq) for g in range(4) for q in range(QUARTERS)]
        first_out = len(GROUPS) * QUARTERS
        first_wq = first_out + 4 * QUARTERS
        last_unit = [PLAN.unit[("proj", g, GROUPS[g][3][-1])] for g in range(len(GROUPS))]
        last_unit += [PLAN.unit[(kind, g, b)] for kind, b in (("out", 1), ("pq", 3)) for g in range(4)]

        def wait_used(eng, n):
            group, q = divmod(n, QUARTERS)
            if q == QUARTERS - 1:
                eng.wait_ge(pj_full, last_unit[group] + 1)
            else:
                eng.wait_ge(w_used, group * (QUARTERS - 1) + q + 1)

        def wait_t_read(eng, t):
            last, count = PLAN.t_read[t]
            eng.wait_ge(t_read[last], count)

        sub_in_q = [sem(f"sub_in{i}") for i in range(4)]

        u_in = [sem(f"u_in{i}") for i in range(OCT)]
        v_in = [sem(f"v_in{i}") for i in range(OCT)]
        u_free, v_free = sem("u_free"), sem("v_free")
        ids_staged = sem("ids_staged")
        slot_seen = sem("slot_seen")
        dots, gelus, weights, diags = sem("dots"), sem("gelus"), sem("weights"), sem("diags")
        alpha_ready = sem("alpha_ready")
        out_done = sem("out_done")
        acc = [tb + db, pj]

        by_key = lambda n: qT[:, n, :].rearrange("p (m k) -> p m k", m=16)
        sv, si, sif = by_key(0), by_key(1).bitcast(U32), by_key(2)
        fv = qT[:, 3, 0:PICKS].rearrange("p (m k) -> p m k", m=8)
        fi = qT[:, 3, PICKS:].bitcast(U32).rearrange("p (m k) -> p m k", m=8)
        by_half = lambda n: qT[:, n, :].rearrange("p (s m k) -> p s m k", s=2, m=8)
        fab, fabf, ex = by_half(4).bitcast(U32), by_half(5), by_half(6)
        gsum = qT[:, 7, 0:16].rearrange("p (s m) -> p s m", s=2)
        cand = at("cand", [8, 16, 16], r_hT)
        eq = at("eq", [8, 16, 16], r_hT + 8 * KB)

        block = ctx.enter_context(nc.Block())

        @block.sync
        def _(sp):
            sp.dma_start(h[:, 0, :], x[0:P, :]).then_inc(x_in[0], 16)
            sp.dma_start(gb[:, 0, :], ln_in_g.partition_broadcast(P)).then_inc(gb_in, 16)
            sp.dma_start(gb[:, 1, :], ln_in_b.partition_broadcast(P)).then_inc(gb_in, 16)
            sp.dma_start(h[:, 1, :], x[P:TOK, :]).then_inc(x_in[1], 16)
            sp.dma_start(ident[:, :], ident_c).then_inc(consts_in, 16)
            sp.dma_start(xm, meta).then_inc(x_in[2], 16)
            sp.dma_start(iota16[:, :], iota_c).then_inc(consts_in, 16)
            sp.dma_start(sink[:, :], sinks.partition_broadcast(P)).then_inc(consts_in, 16)
            for n, (src, c0, cols, q) in enumerate(loads):
                if n >= NRAW:
                    sp.wait_ge(lo_done, n - NRAW + 1)
                sp.dma_start(w_raw[:, n % NRAW, :, 0:cols],
                             src[q * QK * P:(q + 1) * QK * P, c0:c0 + cols]
                             .rearrange("(k p) c -> p k c", p=P)).then_inc(raw_in[n % NRAW], 16)
                if n == NRAW + NSPLIT - 1:
                    sp.wait_ge(ln_done, 3)
                    sp.dma_start(consts_sb[:, :], consts).then_inc(tables_in, 16)
                    for tile in range(TILES):
                        sp.dma_start(h_saved[tile * P:(tile + 1) * P, :], h[:, tile, :]).then_inc(saved, 16)
                if n == first_out + NSPLIT + 2:
                    sp.wait_ge(d_full, PLAN.d[("retO", 3)][0] + 1)
                    sp.wait_ge(ret_gated, 4)
                    sp.wait_ge(saved, 32)
                    for tile in range(TILES):
                        sp.dma_start(h[:, tile, :], h_saved[tile * P:(tile + 1) * P, :]).then_inc(back, 16)
                    sp.dma_start(gb[:, 0, :], ln_mix_g.partition_broadcast(P)).then_inc(gb_in, 16)
                    sp.dma_start(gb[:, 1, :], ln_mix_b.partition_broadcast(P)).then_inc(gb_in, 16)
                if n == first_wq + NRAW:
                    for sub in range(4):
                        if sub:
                            sp.wait_ge(t_full, PLAN.t[("subT", sub - 1)][0] + 1)
                        else:
                            sp.wait_ge(pj_full, PLAN.unit[("out", 3, 1)] + 1)
                        sp.dma_start(subn[:, :, :], subkeys[:, 4 * sub:4 * sub + 4, :]).then_inc(sub_in_q[sub], 16)

            sp.wait_ge(pj_full, len(PLAN.freed))
            sp.dma_start(gb_last[:, 0, :], ln_ffn_g.partition_broadcast(P)).then_inc(gb_in, 16)
            sp.dma_start(gb_last[:, 1, :], ln_ffn_b.partition_broadcast(P)).then_inc(gb_in, 16)
            for tile in range(TILES):
                sp.wait_ge(ln_done, 6 + tile)
                sp.dma_start(out[tile * P:(tile + 1) * P, :], h[:, tile, :]).then_inc(out_done, 16)
            sp.wait_ge(out_done, 32)

        @block.tensor
        def _(pe):
            def unit_bank(u):
                if u >= 4:
                    for e, n in PLAN.freed[u - 4].items():
                        pe.wait_ge(pj_read[e], n)
                return pj[u % 4]

            def t_bank(t):
                if t >= 2:
                    wait_t_read(pe, t - 2)
                return tb[t % 2]

            def d_bank(d):
                if d >= 2:
                    pe.wait_ge(d_read, d - 1)
                return db[d % 2]

            def product(units, group, q0, q1, lhs, rows_of, cols):
                for q in range(q0, q1):
                    n = group * QUARTERS + q
                    slot = n % NSPLIT
                    pe.wait_ge(lo_done, n + 1)
                    for b, u in units:
                        bank = (unit_bank(u) if q == 0 else pj[u % 4])[0:rows_of(b), 0:cols]
                        for k in range(QK):
                            kk = q * QK + k
                            hi, lo = lhs(b, kk)
                            wh, wl = w_hi[:, slot, k, 0:cols], w_lo[:, slot, k, 0:cols]
                            nc.tensor.matmul(bank, hi, wh, start=kk == 0, stop=False)
                            nc.tensor.matmul(bank, hi, wl, start=False, stop=False)
                            last = nc.tensor.matmul(bank, lo, wh, start=False, stop=kk == KC - 1)
                        if q == QUARTERS - 1:
                            last.then_inc(pj_full, 1)
                    if q < QUARTERS - 1:
                        last.then_inc(w_used, 1)

            for job in SCHED:
                kind = job[0]
                if kind == "lnT":
                    b = job[1] if job[1] < 3 else job[1] - 3
                    if job[1] == 0:
                        pe.wait_ge(consts_in, 48)
                    pe.wait_ge(ln_done, job[1] + 1)
                    if b == 2:
                        bank = t_bank(PLAN.t[job][0])
                        for k in range(KC):
                            last = nc.tensor.matmul(bank[:, k * META:(k + 1) * META], xm[:, k * P:(k + 1) * P],
                                                    ident[0:META, 0:META], start=True, stop=True)
                        last.then_inc(t_full, 1)
                    else:
                        for q, t in enumerate(PLAN.t[job]):
                            bank = t_bank(t)
                            for k in range(4):
                                kk = 4 * q + k
                                last = nc.tensor.transpose(bank[:, k * P:(k + 1) * P],
                                                           h[:, b, kk * P:(kk + 1) * P], ident[:, :])
                            last.then_inc(t_full, 1)
                elif kind == "proj":
                    g = job[1]
                    if g == 0:
                        wait_t_read(pe, PLAN.t[("lnT", 2)][0])
                    product([(b, PLAN.unit[("proj", g, b)]) for b in GROUPS[g][3]], g, 0, QUARTERS,
                            lambda b, kk: [t[:, kk, spots[b][0]:spots[b][1]] for t in (hT, hT_lo)], rows, GROUPS[g][2])
                elif kind == "rope":
                    _, g, b = job
                    t = PLAN.t[job][0]
                    pe.wait_ge(stage_full, PLAN.stage[job] + 1)
                    bank = t_bank(t)
                    src = stage[:, PLAN.stage[job] % 2, :]
                    n = rows(b)
                    for c in range(2 if g == 2 else 4):
                        if b == 2:
                            last = nc.tensor.matmul(bank[:, c * META:(c + 1) * META], src[0:META, c * P:(c + 1) * P],
                                                    ident[0:META, 0:META], start=True, stop=True)
                        else:
                            last = nc.tensor.transpose(bank[:, c * P:(c + 1) * P], src[:, c * P:(c + 1) * P], ident[:, :])
                    last.then_inc(t_full, 1)
                elif kind == "attS":
                    _, g, tile = job
                    if (g, tile) == (0, 0):
                        wait_t_read(pe, PLAN.t[("rope", 2, 2)][0])
                    for i, d in enumerate(PLAN.d[job]):
                        bank = d_bank(d)
                        e = i % 2
                        for j in range(2):
                            last = nc.tensor.matmul(bank[:, j * nkeys[tile]:(j + 1) * nkeys[tile]],
                                                    qT[64 * e:64 * e + 64, 4 * g + 2 * (i // 2) + j, tile * P:(tile + 1) * P],
                                                    kT[64 * e:64 * e + 64, g, lo[tile]:lo[tile] + nkeys[tile]],
                                                    start=True, stop=True)
                        last.then_inc(d_full, 1)
                elif kind == "attO":
                    _, g, tile = job
                    n = 2 * g + tile
                    pe.wait_ge(soft_prob, n + 1)
                    n0 = META if tile == 0 else P
                    out_bank = None

                    def pv(pair):
                        wait_t_read(pe, PLAN.t[job][pair])
                        for e in range(2):
                            o = out_bank[64 * e:64 * e + 64, pair * P:(pair + 1) * P]
                            nc.tensor.matmul(o, av[0:n0, 2 if tile == 0 else 0, 64 * g:64 * g + 64],
                                             pT[0:n0, pair % 2, 2 * e, :], start=True, stop=False)
                            last = nc.tensor.matmul(o, av[:, tile, 64 * g:64 * g + 64],
                                                    pT[:, pair % 2, 2 * e + 1, :], start=False, stop=True)
                        return last

                    for pair, t in enumerate(PLAN.t[job]):
                        bank = t_bank(t)
                        for e in range(2):
                            src = prob[:, 2 * pair + e, :]
                            if tile == 0:
                                nc.tensor.matmul(bank[0:META, 2 * e * P:(2 * e + 1) * P], src[:, 0:META], ident[:, :],
                                                 start=True, stop=True)
                            else:
                                nc.tensor.transpose(bank[:, 2 * e * P:(2 * e + 1) * P], src[:, 0:P], ident[:, :])
                            last = nc.tensor.transpose(bank[:, (2 * e + 1) * P:(2 * e + 2) * P], src[:, n0:n0 + P], ident[:, :])
                        last.then_inc(t_full, 1)
                        if pair == 1:
                            out_bank = d_bank(PLAN.d[job][0])
                        if pair >= 1:
                            pv(pair - 1)
                    pv(3).then_inc(d_full, 1)
                elif kind == "retS":
                    hd = job[1]
                    c = 2 * (hd % 2)
                    d0, d1 = PLAN.d[job]
                    wait_t_read(pe, PLAN.t[("rope", 4 if hd < 2 else 8, 2)][0])
                    bank = d_bank(d0)
                    for k in range(2):
                        nc.tensor.matmul(bank[:, 0:TOK], rkT[:, c + k, META:META + P], rqT[:, c + k, :],
                                         start=k == 0, stop=k == 1)
                    for k in range(2):
                        last = nc.tensor.matmul(bank[:, TOK:TOK + P], rkT[:, c + k, META + P:KEYS], rqT[:, c + k, P:TOK],
                                                start=k == 0, stop=k == 1)
                    last.then_inc(d_full, 1)
                    bank = d_bank(d1)
                    for k in range(2):
                        last = nc.tensor.matmul(bank[0:META, 0:TOK], rkT[:, c + k, 0:META], rqT[:, c + k, :],
                                                start=k == 0, stop=k == 1)
                    last.then_inc(d_full, 1)
                elif kind == "retO":
                    hd = job[1]
                    pe.wait_ge(d_read, PLAN.d[("retS", hd)][1] + 1)
                    pe.wait_ge(pj_read["act"], PLAN.freed[PLAN.unit[("proj", 5 if hd < 2 else 9, 2)]]["act"])
                    bank = d_bank(PLAN.d[job][0])
                    v = lambda b: rv[0:rows(b), b, (hd % 2) * RHD:(hd % 2 + 1) * RHD]
                    nc.tensor.matmul(bank[:, 0:RHD], sT[0:META, 3 * P:4 * P], v(2), start=True, stop=False)
                    nc.tensor.matmul(bank[:, 0:RHD], sT[:, 0:P], v(0), start=False, stop=True)
                    nc.tensor.matmul(bank[:, RHD:2 * RHD], sT[0:META, 4 * P:5 * P], v(2), start=True, stop=False)
                    nc.tensor.matmul(bank[:, RHD:2 * RHD], sT[:, P:2 * P], v(0), start=False, stop=False)
                    nc.tensor.matmul(bank[:, RHD:2 * RHD], sT[:, 2 * P:3 * P], v(1), start=False,
                                     stop=True).then_inc(d_full, 1)
                elif kind == "retT":
                    hd = job[1]
                    pe.wait_ge(ret_gated, hd + 1)
                    bank = t_bank(PLAN.t[job][0])
                    for tile in range(TILES):
                        for c in range(2):
                            i = 2 * tile + c
                            last = nc.tensor.transpose(bank[:, i * P:(i + 1) * P], gated[:, tile, c * P:(c + 1) * P], ident[:, :])
                    last.then_inc(t_full, 1)
                elif kind == "subT":
                    q = job[1]
                    pe.wait_ge(sub_in_q[q], 16)
                    bank = t_bank(PLAN.t[job][0])
                    for c in range(4):
                        last = nc.tensor.transpose(bank[:, c * P:(c + 1) * P], subn[:, c, :], ident[:, :])
                    last.then_inc(t_full, 1)
                elif kind == "out":
                    _, g, q0, q1 = job
                    if g == 0:
                        wait_t_read(pe, PLAN.t[("retT", 1 if q0 == 0 else 3)][0])
                        pe.wait_ge(d_read, PLAN.d[("attO", 1, 1)][0] + 1)
                    product([(b, PLAN.unit[("out", g, b)]) for b in range(TILES)], len(GROUPS) + g, q0, q1,
                            lambda b, kk: [t[:, kk, b * P:(b + 1) * P] for t in (mixT, mixT_lo)], rows, GCOLS)
                elif kind == "pq":
                    g = job[1]
                    if g == 0:
                        wait_t_read(pe, PLAN.t[("lnT", 4)][3])
                    for q in range(QUARTERS):
                        n = (len(GROUPS) + 4 + g) * QUARTERS + q
                        slot = n % NSPLIT
                        pe.wait_ge(lo_done, n + 1)
                        for b in range(4):
                            u = PLAN.unit[("pq", g, b)]
                            bank = (unit_bank(u) if q == 0 else pj[u % 4])[:, 0:TOK]
                            for k in range(QK):
                                kk = q * QK + k
                                wh, wl = (t[:, slot, k, b * P:(b + 1) * P] for t in (w_hi, w_lo))
                                nc.tensor.matmul(bank, wh, hT[:, kk, 0:TOK], start=kk == 0, stop=False)
                                nc.tensor.matmul(bank, wh, hT_lo[:, kk, 0:TOK], start=False, stop=False)
                                last = nc.tensor.matmul(bank, wl, hT[:, kk, 0:TOK], start=False, stop=kk == KC - 1)
                            if q == QUARTERS - 1:
                                last.then_inc(pj_full, 1)
                        if q < QUARTERS - 1:
                            last.then_inc(w_used, 1)
                elif kind == "ps":
                    tile = job[1]
                    if tile == 0:
                        pe.wait_ge(pj_read["act"], PLAN.freed[PLAN.unit[("pq", 3, 3)]]["act"])
                        wait_t_read(pe, PLAN.t[("subT", 3)][0])
                    for b in range(4):
                        bank = unit_bank(PLAN.unit[("ps", tile, b)])
                        for c in range(4):
                            m = 4 * b + c
                            last = nc.tensor.matmul(bank[:, c * P:(c + 1) * P], pqT[:, m, tile * P:(tile + 1) * P],
                                                    skT[:, m, :], start=True, stop=True)
                        last.then_inc(pj_full, 1)

            pe.wait_ge(alpha_ready, 1)
            for e in ("act", "dve"):
                pe.wait_ge(t_read[e], max(n for last, n in PLAN.t_read if last == e))
            pe.wait_ge(d_read, sum(map(len, PLAN.d.values())))
            for tile in range(TILES):
                if tile == 1:
                    pe.wait_ge(pj_read["act"], PLAN.freed[-1]["act"])
                for c in range(4):
                    nc.tensor.matmul(acc[tile][c][:, :], alphaI[:, :], h[:, tile, c * 512:(c + 1) * 512],
                                     start=True, stop=False, skip_group_check=True)
                with pe.Fori(0, STEPS) as i:
                    n = i + tile * STEPS
                    pe.wait_ge(diags, n + 1)
                    for k in range(OCT):
                        pe.wait_ge(v_in[k], (n + 1) * 16)
                        for c in range(4):
                            last = nc.tensor.matmul(acc[tile][c][:, :], diag[:, k, :], V[:, k, c * 512:(c + 1) * 512],
                                                    start=False, stop=False, skip_group_check=True)
                        last.then_inc(v_free, 1)

        @block.scalar
        def _(act):
            steps = [0]

            def link(ins):
                steps[0] += 1
                ins.then_inc(act_step, 1)
                act.wait_ge(act_step, steps[0])

            def norm_sqrt(n):
                act.wait_ge(norm_var, n + 1)
                nc.scalar.activation(rstd[:, 0:1], rstd[:, 0:1], ACT.Sqrt).then_inc(norm_sd, 1)

            def gate_exp(tile, part):
                act.wait_ge(fexp_in, tile * PARTS + part + 1)
                quarter = gates[:, tile, part * PICKS // PARTS:(part + 1) * PICKS // PARTS]
                nc.scalar.activation(quarter, quarter, ACT.Exp).then_inc(fexp_out, 1)

            rounded = [0]

            def round_weights(until):
                for n in range(rounded[0], min(until, len(loads))):
                    act.wait_ge(raw_in[n % NRAW], 16 * (n // NRAW + 1))
                    if n >= NSPLIT:
                        wait_used(act, n - NSPLIT)
                    cols = loads[n][2]
                    nc.scalar.copy(w_hi[:, n % NSPLIT, :, 0:cols], w_raw[:, n % NRAW, :, 0:cols]).then_inc(hi_done, 1)
                    rounded[0] = n + 1

            for job in SCHED:
                kind = job[0]
                if kind == "lnT" and job[1] == 2:
                    round_weights(NSPLIT)
                elif kind == "proj":
                    round_weights((job[1] + 1) * QUARTERS + NSPLIT)
                elif kind == "out":
                    round_weights((len(GROUPS) + job[1]) * QUARTERS + job[3] + NSPLIT)
                elif kind == "pq":
                    round_weights((len(GROUPS) + 4 + job[1] + 1) * QUARTERS + NSPLIT)
                if kind == "lnT":
                    b = job[1] if job[1] < 3 else job[1] - 3
                    if job[1] in (0, 3):
                        norm_sqrt(job[1])
                        norm_sqrt(job[1] + 1)
                    elif job[1] == 2:
                        norm_sqrt(job[1])
                    if job[1] == 3:
                        act.wait_ge(pj_full, PLAN.unit[("proj", 10, 1)] + 1)
                    for q, t in enumerate(PLAN.t[job]):
                        act.wait_ge(t_full, t + 1)
                        if b == 2:
                            dst, src = hT[:, :, TOK:KEYS], tb[t % 2][:, 0:KC * META].rearrange("p (k n) -> p k n", k=KC)
                        else:
                            dst = hT[:, 4 * q:4 * q + 4, spots[b][0]:spots[b][1]]
                            src = tb[t % 2][:, :].rearrange("p (k n) -> p k n", k=4)
                        nc.scalar.copy(dst, src).then_inc(t_hi, 1)
                elif kind == "rope":
                    _, g, b = job
                    t = PLAN.t[job][0]
                    gk = GROUPS[g][0]
                    if gk == "rq" and g == 3 and b == 0:
                        act.wait_ge(saved, 32)
                    if gk == "rq" and g == 7 and b == 0:
                        act.wait_ge(d_full, PLAN.d[("retS", 1)][1] + 1)
                    act.wait_ge(t_full, t + 1)
                    n = rows(b)
                    nch = 2 if gk == "akv" else 4
                    src = tb[t % 2][:, 0:nch * n].rearrange("p (c n) -> p c n", c=nch)
                    k0, k1 = keyspots[b]
                    dst = {"aq": lambda: qT[:, 4 * g:4 * g + 4, b * P:(b + 1) * P],
                           "akv": lambda: kT[:, :, k0:k1],
                           "rq": lambda: rqT[:, :, b * P:(b + 1) * P],
                           "rk": lambda: rkT[:, :, k0:k1]}[gk]()
                    nc.scalar.copy(dst, src).then_inc(t_read["act"], 1)
                elif kind == "copy":
                    _, g, b = job
                    u = PLAN.unit[("proj", g, b)]
                    act.wait_ge(pj_full, u + 1)
                    if g == 9 and b == 0:
                        act.wait_ge(d_full, PLAN.d[("retO", 1)][0] + 1)
                    if g == 10 and b == 0:
                        act.wait_ge(ret_gated, 2)
                    n = rows(b)
                    if GROUPS[g][0] == "akv":
                        act.wait_ge(pj_read["dve"], PLAN.freed[u]["dve"])
                        nc.scalar.copy(av[0:n, b, :], pj[u % 4][0:n, P:2 * P]).then_inc(pj_read["act"], 1)
                    elif GROUPS[g][0] == "rv":
                        nc.scalar.copy(rv[0:n, b, :], pj[u % 4][0:n, :]).then_inc(pj_read["act"], 1)
                    else:
                        nc.scalar.activation(rg[:, b, :], pj[u % 4][:, :], ACT.Silu).then_inc(pj_read["act"], 1)
                elif kind == "attS":
                    _, g, tile = job
                    n = 2 * g + tile
                    act.wait_ge(soft_max, n + 1)
                    for e in range(8):
                        nc.scalar.activation(prob[:, e, 0:nkeys[tile]], prob[:, e, 0:nkeys[tile]], ACT.Exp,
                                             bias=mx[:, 0, e:e + 1], accum_out=mx[:, 2, e:e + 1])
                    nc.scalar.activation(mx[:, 1, :], mx[:, 1, :], ACT.Exp).then_inc(soft_exp, 1)
                elif kind == "attO":
                    _, g, tile = job
                    n0 = META if tile == 0 else P
                    for pair, t in enumerate(PLAN.t[job]):
                        act.wait_ge(t_full, t + 1)
                        src = tb[t % 2][:, :].rearrange("p (e k n) -> p e k n", e=2, k=2)
                        dst = pT[:, pair % 2, :, :].rearrange("p (e k) n -> p e k n", e=2)
                        if tile == 0:
                            nc.scalar.copy(dst[0:META, :, 0, :], src[0:META, :, 0, :])
                            nc.scalar.copy(dst[:, :, 1, :], src[:, :, 1, :]).then_inc(t_read["act"], 1)
                        else:
                            nc.scalar.copy(dst, src).then_inc(t_read["act"], 1)
                elif kind == "retO":
                    act.wait_ge(gvar, job[1] + 1)
                    nc.scalar.activation(gn[:, 1, :], gn[:, 1, :], ACT.Sqrt).then_inc(gsd, 1)
                elif kind == "retT":
                    hd = job[1]
                    t = PLAN.t[job][0]
                    act.wait_ge(t_full, t + 1)
                    c0 = 8 + 2 * hd
                    nc.scalar.copy(mixT[:, c0:c0 + 2, :].rearrange("p c (t n) -> p t c n", t=2),
                                   tb[t % 2][:, :].rearrange("p (t c n) -> p t c n", t=2, c=2)).then_inc(t_hi, 1)
                elif kind == "subT":
                    t = PLAN.t[job][0]
                    act.wait_ge(t_full, t + 1)
                    nc.scalar.copy(skT[:, 4 * job[1]:4 * job[1] + 4, :],
                                   tb[t % 2][:, :].rearrange("p (c n) -> p c n", c=4)).then_inc(t_read["act"], 1)
                elif kind == "pq":
                    for b in range(4):
                        u = PLAN.unit[("pq", job[1], b)]
                        act.wait_ge(pj_full, u + 1)
                        nc.scalar.copy(pqT[:, 4 * job[1] + b, :], pj[u % 4][:, 0:TOK]).then_inc(pj_read["act"], 1)
                elif kind == "ps":
                    tile = job[1]
                    if tile == 1:
                        for part in range(PARTS):
                            gate_exp(0, part)
                        act.wait_ge(keys_taken, PARTS)
                    for b in range(4):
                        u = PLAN.unit[("ps", tile, b)]
                        act.wait_ge(pj_full, u + 1)
                        nc.scalar.copy(work[:, b * 512:(b + 1) * 512], pj[u % 4][:, :]).then_inc(pj_read["act"], 1)

            for tile in range(TILES):
                for part in range(PARTS if tile == 0 else 1):
                    steps_here = STEPS // PARTS if tile == 0 else STEPS
                    with act.Fori(0, steps_here) as i:
                        n = i + tile * STEPS + part * steps_here
                        act.wait_ge(u_free, (n + 2) * OCT)
                        nc.scalar.activation(ga[:, :], dot[:, :], ACT.Gelu).then_inc(gelus, 1)
                    if tile == 0:
                        gate_exp(1, part)
                act.wait_ge(norm_var, 6 + tile)
                nc.scalar.activation(rstd[:, 0:1], rstd[:, 0:1], ACT.Sqrt).then_inc(norm_sd, 1)

        dve_steps = [0]

        def link(ins):
            dve_steps[0] += 1
            ins.then_inc(dve_step, 1)
            nc.vector.wait_ge(dve_step, dve_steps[0])

        def layer_norm(t, n, number, gb, st, taken=False):
            if not taken:
                for c in range(4):
                    last = nc.vector.bn_stats(st[0:n, c, :], t[:, c * 512:(c + 1) * 512])
                link(last)
            link(nc.vector.bn_aggr(mv[0:n, :], st[0:n, :, :].rearrange("p a b -> p (a b)")))
            if n < P:
                link(nc.vector.memset(rstd[:, 0:1], 1.0))
            nc.vector.tensor_scalar_add(rstd[0:n, 0:1], mv[0:n, 1:2], LN_EPS).then_inc(norm_var, 1)
            nc.vector.wait_ge(norm_sd, number + 1)
            link(nc.vector.reciprocal(rstd[0:n, 1:2], rstd[0:n, 0:1]))
            link(nc.vector.tensor_scalar(t, t, mv[0:n, 0:1], rstd[0:n, 1:2], ALU.subtract, ALU.mult))
            link(nc.vector.tensor_tensor(t, t, gb[0:n, 0, :], ALU.mult))
            nc.vector.tensor_tensor(t, t, gb[0:n, 1, :], ALU.add).then_inc(ln_done, 1)

        @block.vector
        def _(dve):
            def picks(tile, part):
                if part == 0:
                    dve.wait_ge(pj_read["act"], PLAN.freed[PLAN.unit[("ps", tile, 3)]]["act"])
                n = tile * PARTS + part
                s3 = work[:, :].rearrange("p (m n) -> p m n", m=16)
                m0, m1 = 4 * part, 4 * part + 4
                for m in range(m0, m1):
                    link(nc.vector.max(sv[:, m, 0:8], s3[:, m, :]))
                    nc.vector.max_index(si[:, m, 0:8], sv[:, m, 0:8], s3[:, m, :])
                    link(nc.vector.match_replace(sc2[:, :], sv[:, m, 0:8], s3[:, m, :], -3e38))
                    link(nc.vector.max(sv[:, m, 8:16], sc2[:, :]))
                    link(nc.vector.max_index(si[:, m, 8:16], sv[:, m, 8:16], sc2[:, :]))
                nc.vector.tensor_copy(sif[:, m0:m1, :], si[:, m0:m1, :]).then_inc(keys_taken, 1)
                dve.wait_ge(keys_taken, n + 1)
                h0, h1 = 2 * part, 2 * part + 2
                halves_of = lambda t: t[:, m0:m1, :].rearrange("p (m s) k -> p m s k", s=2)
                grid = [P, 2, 16, 16]
                svp, sifp = halves_of(sv), halves_of(sif)
                c, e = cand[:, h0:h1, :, :], eq[:, h0:h1, :, :]
                link(nc.vector.tensor_tensor(c, svp[:, :, 0, :].unsqueeze(3).to_broadcast(grid),
                                             svp[:, :, 1, :].unsqueeze(2).to_broadcast(grid), ALU.add))
                cflat, eflat = c.rearrange("p m a b -> p m (a b)"), e.rearrange("p m a b -> p m (a b)")
                for m in range(2):
                    best, where = fv[:, h0 + m, :], fi[:, h0 + m, :]
                    link(nc.vector.max(best[:, 0:8], cflat[:, m, :]))
                    nc.vector.max_index(where[:, 0:8], best[:, 0:8], cflat[:, m, :])
                    link(nc.vector.match_replace(eflat[:, m, :], best[:, 0:8], cflat[:, m, :], -3e38))
                    link(nc.vector.max(best[:, 8:16], eflat[:, m, :]))
                    link(nc.vector.max_index(where[:, 8:16], best[:, 8:16], eflat[:, m, :]))
                gv = gates[:, tile, :].rearrange("p (m k) -> p m k", m=8)[:, h0:h1, :]
                nc.vector.tensor_tensor(gv, fv[:, h0:h1, :], fv[:, h0:h1, 0:1].to_broadcast([P, 2, 16]),
                                        ALU.subtract).then_inc(fexp_in, 1)
                nc.vector.tensor_single_scalar(fab[:, 0, h0:h1, :], fi[:, h0:h1, :], 4, ALU.logical_shift_right)
                link(nc.vector.tensor_single_scalar(fab[:, 1, h0:h1, :], fi[:, h0:h1, :], 15, ALU.bitwise_and))
                link(nc.vector.tensor_copy(fabf[:, :, h0:h1, :], fab[:, :, h0:h1, :]))
                for s in range(2):
                    link(nc.vector.tensor_tensor(e, fabf[:, s, h0:h1, :].unsqueeze(3).to_broadcast(grid),
                                                 iota16[:, :].unsqueeze(1).unsqueeze(1).to_broadcast(grid),
                                                 ALU.is_equal))
                    link(nc.vector.tensor_tensor(e, e, sifp[:, :, s, :].unsqueeze(2).to_broadcast(grid), ALU.mult))
                    link(nc.vector.reduce_sum(ex[:, s, h0:h1, :], e, AX.X))
                link(nc.vector.scalar_tensor_tensor(
                    out=ids[:, tile, :].rearrange("p (m k) -> p m k", m=8)[:, h0:h1, :], in0=ex[:, 0, h0:h1, :],
                    scalar=float(NKEY), in1=ex[:, 1, h0:h1, :], op0=ALU.mult, op1=ALU.add))
                dve.wait_ge(fexp_out, n + 1)
                link(nc.vector.reduce_sum(gsum[:, 0, h0:h1], gv, AX.X))
                link(nc.vector.reciprocal(gsum[:, 1, h0:h1], gsum[:, 0, h0:h1]))
                nc.vector.tensor_tensor(gv, gv, gsum[:, 1, h0:h1].unsqueeze(2).to_broadcast([P, 2, 16]),
                                        ALU.mult).then_inc(picks_ready, 1)

            def rope(src, dst, heads, half, cos, sin, n, twice):
                r = lambda a: a[0:n, 0:heads * 2 * half].rearrange("p (a s c) -> p a s c", a=heads, s=2)
                bc = lambda tab: tab.unsqueeze(1).unsqueeze(1).to_broadcast([n, heads, 2, half])
                a, b = r(ropeA), r(ropeB)
                s4 = src.rearrange("p (a s c) -> p a s c", a=heads, s=2)
                nc.vector.tensor_tensor(a, s4, bc(cos), ALU.mult)
                ins = nc.vector.tensor_tensor(b, s4, bc(sin), ALU.mult)
                ins.then_inc(pj_read["dve"], 1)
                return a, b

            for job in SCHED:
                kind = job[0]
                if kind == "lnT":
                    j = job[1]
                    b = j if j < 3 else j - 3
                    if j == 0:
                        for tile in range(TILES):
                            dve.wait_ge(x_in[tile], 16)
                            if tile == 0:
                                dve.wait_ge(gb_in, 32)
                            layer_norm(h[:, tile, :], P, tile, gb, stats[:, tile, :, :])
                    elif j == 2:
                        dve.wait_ge(x_in[2], 16)
                        layer_norm(xm, META, j, gb, stats[:, 0, :, :])
                    elif j == 3:
                        dve.wait_ge(gb_in, 64)
                        for tile in range(TILES):
                            layer_norm(h[:, tile, :], P, 3 + tile, gb, stats[:, tile, :, :], taken=True)
                    for q, t in enumerate(PLAN.t[job]):
                        dve.wait_ge(t_hi, PLAN.t_split[t] + 1)
                        if b == 2:
                            part = (slice(None), slice(None), slice(TOK, KEYS))
                            src = tb[t % 2][:, 0:KC * META].rearrange("p (k n) -> p k n", k=KC)
                        else:
                            part = (slice(None), slice(4 * q, 4 * q + 4), slice(*spots[b]))
                            src = tb[t % 2][:, :].rearrange("p (k n) -> p k n", k=4)
                        nc.vector.tensor_tensor(hT_lo[part], src, hT[part].bitcast(F32),
                                                ALU.subtract).then_inc(t_read["dve"], 1)
                elif kind == "retT":
                    t = PLAN.t[job][0]
                    part = (slice(None), slice(8 + 2 * job[1], 10 + 2 * job[1]), slice(None))
                    dve.wait_ge(t_hi, PLAN.t_split[t] + 1)
                    nc.vector.tensor_tensor(mixT_lo[part].rearrange("p c (t n) -> p t c n", t=2),
                                            tb[t % 2][:, :].rearrange("p (t c n) -> p t c n", t=2, c=2),
                                            mixT[part].bitcast(F32).rearrange("p c (t n) -> p t c n", t=2),
                                            ALU.subtract).then_inc(t_read["dve"], 1)
                elif kind == "rope":
                    _, g, b = job
                    gk = GROUPS[g][0]
                    u = PLAN.unit[("proj", g, b)]
                    n = rows(b)
                    half = AHD // 2 if gk[0] == "a" else RHD // 2
                    heads = {"aq": 8, "akv": 2, "rq": 2, "rk": 2}[gk]
                    cos, sin = rope_tab(gk, b, n)
                    if g == 0 and b == 0:
                        dve.wait_ge(tables_in, 16)
                    dve.wait_ge(pj_full, u + 1)
                    a, bb = rope(pj[u % 4][0:n, 0:heads * 2 * half], None, heads, half, cos, sin, n, gk == "akv")
                    dve.wait_ge(pj_read["dve"], PLAN.freed[u]["dve"])
                    s = PLAN.stage[job]
                    if s >= 2:
                        dve.wait_ge(t_full, PLAN.stage_t[s - 2] + 1)
                    st = stage[0:n, s % 2, :]
                    if gk == "akv":
                        o = st[:, 0:2 * P].rearrange("p (a t s c) -> p a t s c", a=2, t=2, s=2)
                        for copy in range(2):
                            nc.vector.tensor_tensor(o[:, :, copy, 0, :], a[:, :, 0, :], bb[:, :, 1, :], ALU.subtract)
                            last = nc.vector.tensor_tensor(o[:, :, copy, 1, :], a[:, :, 1, :], bb[:, :, 0, :], ALU.add)
                    else:
                        o = st.rearrange("p (a s c) -> p a s c", a=heads, s=2)
                        nc.vector.tensor_tensor(o[:, :, 0, :], a[:, :, 0, :], bb[:, :, 1, :], ALU.subtract)
                        last = nc.vector.tensor_tensor(o[:, :, 1, :], a[:, :, 1, :], bb[:, :, 0, :], ALU.add)
                    last.then_inc(stage_full, 1)
                    dve.wait_ge(stage_full, s + 1)
                elif kind == "attS":
                    _, g, tile = job
                    n = 2 * g + tile
                    nk = nkeys[tile]
                    if n == 0:
                        dve.wait_ge(consts_in, 48)
                    if n:
                        before = ("attO", (n - 1) // 2, (n - 1) % 2)
                        dve.wait_ge(t_full, PLAN.t[before][3] + 1)
                    for i, d in enumerate(PLAN.d[job]):
                        dve.wait_ge(d_full, d + 1)
                        h0 = 4 * (i // 2) + i % 2
                        nc.vector.scalar_tensor_tensor(
                            out=prob[:, h0:h0 + 3:2, 0:nk],
                            in0=db[d % 2][:, 0:2 * nk].rearrange("p (e k) -> p e k", e=2), scalar=AHD ** -0.5,
                            in1=mask[tile].unsqueeze(1).to_broadcast([P, 2, nk]),
                            op0=ALU.mult, op1=ALU.add).then_inc(d_read, 1)
                    dve.wait_ge(d_read, PLAN.d[job][3] + 1)
                    link(nc.vector.reduce_max(mx[:, 1, :], prob[:, :, 0:nk], AX.X))
                    sk = sink[:, 8 * g:8 * g + 8]
                    link(nc.vector.tensor_tensor(mx[:, 1, :], mx[:, 1, :], sk, ALU.max))
                    link(nc.vector.tensor_scalar_mul(mx[:, 0, :], mx[:, 1, :], -1.0))
                    nc.vector.tensor_tensor(mx[:, 1, :], sk, mx[:, 0, :], ALU.add).then_inc(soft_max, 1)
                    dve.wait_ge(soft_exp, n + 1)
                    link(nc.vector.tensor_tensor(mx[:, 2, :], mx[:, 2, :], mx[:, 1, :], ALU.add))
                    link(nc.vector.reciprocal(mx[:, 2, :], mx[:, 2, :]))
                    nc.vector.tensor_tensor(prob[:, :, 0:nk], prob[:, :, 0:nk],
                                            mx[:, 2, :].unsqueeze(2).to_broadcast([P, 8, nk]),
                                            ALU.mult).then_inc(soft_prob, 1)
                elif kind == "attO":
                    _, g, tile = job
                    d = PLAN.d[job][0]
                    dve.wait_ge(d_full, d + 1)
                    part = (slice(None), slice(4 * g, 4 * g + 4), slice(tile * P, (tile + 1) * P))
                    src = db[d % 2][:, :].rearrange("p (c n) -> p c n", c=4)
                    link(nc.vector.tensor_copy(mixT[part], src))
                    nc.vector.tensor_tensor(mixT_lo[part], src, mixT[part].bitcast(F32),
                                            ALU.subtract).then_inc(d_read, 1)
                elif kind == "retS":
                    hd = job[1]
                    d0, d1 = PLAN.d[job]
                    if hd:
                        dve.wait_ge(d_full, PLAN.d[("retO", hd - 1)][0] + 1)
                    dve.wait_ge(d_full, d0 + 1)
                    nc.vector.tensor_tensor(sT[:, 0:TOK], db[d0 % 2][:, 0:TOK], decay[:, hd, 0, :], ALU.mult)
                    nc.vector.tensor_tensor(sT[:, TOK:TOK + P], db[d0 % 2][:, TOK:TOK + P], decay[:, hd, 0, 0:P],
                                            ALU.mult).then_inc(d_read, 1)
                    dve.wait_ge(d_full, d1 + 1)
                    nc.vector.tensor_tensor(sT[0:META, 3 * P:5 * P], db[d1 % 2][0:META, 0:TOK], decay[0:META, hd, 1, :],
                                            ALU.mult).then_inc(d_read, 1)
                elif kind == "retO":
                    hd = job[1]
                    d = PLAN.d[job][0]
                    dve.wait_ge(d_full, d + 1)
                    if hd:
                        dve.wait_ge(t_full, PLAN.t[("retT", hd - 1)][0] + 1)
                    bank = db[d % 2][:, :].rearrange("p (t e) -> p t e", t=2)
                    for tile in range(TILES):
                        link(nc.vector.bn_stats(stats[:, 0, 0, :], bank[:, tile, :]))
                        link(nc.vector.bn_aggr(mv[:, :], stats[:, 0, 0, :]))
                        link(nc.vector.tensor_copy(gn[:, 0, tile:tile + 1], mv[:, 0:1]))
                        last = nc.vector.tensor_scalar_add(gn[:, 1, tile:tile + 1], mv[:, 1:2], LN_EPS)
                        if tile == 0:
                            link(last)
                    last.then_inc(gvar, 1)
                    dve.wait_ge(gsd, hd + 1)
                    link(nc.vector.reciprocal(gn[:, 1, :], gn[:, 1, :]))
                    for tile in range(TILES):
                        last = nc.vector.tensor_scalar(gated[:, tile, :], bank[:, tile, :], gn[:, 0, tile:tile + 1],
                                                       gn[:, 1, tile:tile + 1], ALU.subtract, ALU.mult)
                    last.then_inc(d_read, 1)
                    dve.wait_ge(d_read, d + 1)
                    dve.wait_ge(pj_read["act"], PLAN.freed[PLAN.unit[("proj", 6 if hd < 2 else 10, 1)]]["act"])
                    nc.vector.tensor_tensor(gated[:, :, :], gated[:, :, :],
                                            rg[:, :, (hd % 2) * RHD:(hd % 2 + 1) * RHD], ALU.mult).then_inc(ret_gated, 1)
                elif kind == "out" and job[3] == QUARTERS:
                    g = job[1]
                    if g == 0:
                        dve.wait_ge(back, 32)
                    for b in range(TILES):
                        u = PLAN.unit[("out", g, b)]
                        dve.wait_ge(pj_full, u + 1)
                        hs = h[:, b, g * GCOLS:(g + 1) * GCOLS]
                        nc.vector.scalar_tensor_tensor(out=hs, in0=hs, scalar=ALPHA, in1=pj[u % 4][:, :],
                                                       op0=ALU.mult, op1=ALU.add).then_inc(pj_read["dve"], 1)
                        dve.wait_ge(pj_read["dve"], PLAN.freed[u]["dve"])
                        link(nc.vector.bn_stats(stats[:, b, g, :], hs))
                elif kind == "ps" and job[1] == 0:
                    for part in range(PARTS):
                        picks(0, part)

            dve.wait_ge(pj_full, len(PLAN.freed))
            nc.vector.tensor_scalar_mul(alphaI[:, :], ident[:, :], ALPHA).then_inc(alpha_ready, 1)
            for tile in range(TILES):
                for part in range(PARTS if tile == 0 else 1):
                    steps_here = STEPS // PARTS if tile == 0 else STEPS
                    with dve.Fori(0, steps_here) as i:
                        step = i + part * steps_here
                        n = step + tile * STEPS
                        for k in range(OCT):
                            dve.wait_ge(u_in[k], (n + 1) * 16)
                            nc.vector.tensor_tensor_reduce(out=U[:, k, :], in0=U[:, k, :], in1=h[:, tile, :], scale=1.0,
                                                           scalar=0.0, op0=ALU.mult, op1=ALU.add,
                                                           accum_out=dot[:, k:k + 1]).then_inc(u_free, 1)
                        dve.wait_ge(gelus, n + 1)
                        nc.vector.tensor_tensor(wg[:, :], ga[:, :], gates[:, tile, bass.ts(step, OCT)],
                                                ALU.mult).then_inc(weights, 1)
                        dve.wait_ge(weights, n + 1)
                        dve.wait_ge(v_free, (n + 1) * OCT)
                        nc.vector.tensor_tensor(diag[:, :, :], ident[:, :].unsqueeze(1).to_broadcast([P, OCT, P]),
                                                wg[:, :].unsqueeze(2).to_broadcast([P, OCT, P]), ALU.mult).then_inc(diags, 1)
                    if tile == 0:
                        picks(1, part)
                dve.wait_ge(v_free, OCT * (1 + (tile + 1) * STEPS))
                for c in range(4):
                    last = nc.vector.tensor_copy(h[:, tile, c * 512:(c + 1) * 512], acc[tile][c][:, :])
                link(last)
                dve.wait_ge(gb_in, 96)
                layer_norm(h[:, tile, :], P, 5 + tile, gb_last, stats[:, tile, :, :])

        @block.gpsimd
        def _(pool):
            for n, (_, _, cols, _) in enumerate(loads):
                pool.wait_ge(hi_done, n + 1)
                nc.gpsimd.tensor_tensor(w_lo[:, n % NSPLIT, :, 0:cols], w_raw[:, n % NRAW, :, 0:cols],
                                        w_hi[:, n % NSPLIT, :, 0:cols].bitcast(F32), ALU.subtract).then_inc(lo_done, 1)

            pool.wait_ge(pj_full, len(PLAN.freed))
            nc.gpsimd.engine_nop().then_inc(u_free, OCT)
            nc.gpsimd.engine_nop().then_inc(v_free, OCT)
            for quarter in range(TILES * PARTS):
                tile, part = divmod(quarter, PARTS)
                pool.wait_ge(picks_ready, quarter + 1)
                with pool.Fori(0, STEPS // PARTS // 2) as i:
                    for turn in range(2):
                        step = i * 2 + turn + part * (STEPS // PARTS)
                        n = step + tile * STEPS
                        nc.gpsimd.tensor_copy(idq[:, turn, :], ids[:, tile, bass.ts(step, OCT)]).then_inc(ids_staged, 1)
                        pool.wait_ge(ids_staged, n + 1)
                        for table, slots, free, land in ((peer_u, U, u_free, u_in), (peer_v, V, v_free, v_in)):
                            for k in range(OCT):
                                pool.wait_ge(free, n * OCT + k + 1)
                                nc.gpsimd.sem_inc(slot_seen, 1)
                                nc.gpsimd.indirect_dma_start(
                                    out=slots[:, k, :], out_offset=None, in_=table,
                                    in_offset=bass.IndirectOffsetOnAxis(ap=idq[:, turn, k:k + 1], axis=0)
                                ).then_inc(land[k], 16)


def constants():
    import numpy as np
    f = np.float32
    c = np.zeros((P, C_END), f)
    for b, first in ((0, META), (1, META + P), (2, 0)):
        pos = (first + np.arange(P)).astype(f)
        for dh, o in ((AHD, C_ROPE_A), (RHD, C_ROPE_R)):
            inv = f(10000.0) ** (-np.arange(0, dh, 2, dtype=f) / f(dh))
            ang = (pos[:, None] * inv[None, :]).astype(f)
            w = dh // 2
            c[:, o + b * dh:o + b * dh + w] = np.cos(ang.astype(np.float64))
            c[:, o + b * dh + w:o + (b + 1) * dh] = np.sin(ang.astype(np.float64))
    i = np.arange(P)[:, None]
    for o, lo, keys, tile in ((C_MASK, 0, META + P, 0), (C_MASK + META + P, META, TOK, 1)):
        diff = (META + tile * P + i) - (lo + np.arange(keys)[None, :])
        c[:, o:o + keys] = np.where((diff >= 0) & (diff < 128), 0.0, NEG)
    q = np.arange(TOK)[None, :]
    for hd in range(RET_HEADS):
        g = 1.0 - 2.0 ** (-5.0 - hd)
        own = np.where(q - i >= 0, g ** np.maximum(q - i, 0).astype(np.float64), 0.0)
        met = g ** (q + META - i).astype(np.float64)
        o = C_DECAY + hd * 2 * TOK
        c[:, o:o + TOK] = own * RHD ** -0.5
        c[:, o + TOK:o + 2 * TOK] = met * RHD ** -0.5
    return c, np.eye(P, dtype=f), np.tile(np.arange(TOPK, dtype=f), (P, 1))


def kernel(x, meta_tokens, ln_in_g, ln_in_b, w_in, att_sinks, w_out, ln_mix_g, ln_mix_b,
           peer_wq, peer_subkeys, peer_u, peer_v, ln_ffn_g, ln_ffn_b):
    import numpy as np
    import concourse.bacc as bacc
    from concourse.bass_utils import run_bass_kernel_spmd

    nc = bacc.Bacc("TRN2", target_bir_lowering=False, num_devices=1)
    consts, ident, iota = constants()
    given = {
        "x": np.asarray(x)[0], "meta": meta_tokens, "ln_in_g": ln_in_g, "ln_in_b": ln_in_b,
        "w_in": np.asarray(w_in)[0], "sinks": np.asarray(att_sinks)[0], "w_out": np.asarray(w_out)[0],
        "ln_mix_g": np.asarray(ln_mix_g)[0], "ln_mix_b": np.asarray(ln_mix_b)[0],
        "wq": np.asarray(peer_wq)[0],
        "subkeys": np.asarray(peer_subkeys)[0].reshape(2 * PH, NKEY, P).transpose(1, 0, 2),
        "peer_u": np.asarray(peer_u)[0], "peer_v": np.asarray(peer_v)[0],
        "ln_ffn_g": np.asarray(ln_ffn_g)[0], "ln_ffn_b": np.asarray(ln_ffn_b)[0],
        "consts": consts, "ident_c": ident, "iota_c": iota,
    }
    arrays, args = {}, []
    for name, value in given.items():
        arrays["in_" + name] = a = np.ascontiguousarray(value)
        args.append(nc.dram_tensor("in_" + name, a.shape, mybir.dt.from_np(a.dtype), kind="ExternalInput").ap())
    out = nc.dram_tensor("layer_out", (TOK, D), F32, kind="ExternalOutput").ap()
    build(nc, *args, out)
    r = run_bass_kernel_spmd(nc, [arrays], core_ids=[0])
    return np.asarray(r.results[0]["layer_out"]).reshape(1, TOK, D)
```

```python
import math
from contextlib import ExitStack

import concourse.bass as bass
from concourse import mybir

F32 = mybir.dt.float32
F32R = mybir.dt.float32r
U32 = mybir.dt.uint32
ALU = mybir.AluOpType
ACT = mybir.ActivationFunctionType
AX = mybir.AxisListType

P = 128
D = 2048
KC = D // P
META = 16
TILES = 2
TOK = TILES * P
KEYS = META + TOK
GCOLS = 512
QK = 2
LOADS = KC // QK
LATE = 3 * LOADS // 4
NRAW, NSPLIT = 4, 6
STAGES = 3
AQ_HEADS, AHD = 16, 64
RET_HEADS, RHD = 4, 256
COL_AK = AQ_HEADS * AHD
COL_RET = COL_AK + 4 * AHD
LN_EPS = 1e-5
ALPHA = 2.0 ** 0.25
NEG = -1e30
NORM_TILES = (TILES, 1, TILES, TILES)
PH, TOPK, NKEY = 8, 16, 128
PICKS = PH * TOPK
PARTS = PH
SLOTS = (8, 4)
OCT = 8
TURNS = TOPK // OCT
GROUP = 4
PAIR = GROUP // 2
BANKS = 4
GRID_BANKS = 2
ROUNDS = P // (BANKS * GROUP)
FILLS = BANKS * 2
POOL_FILLS = (3, 7)
HOT_SLOTS = 3
V_RAW, V_SPLIT = 4, 2

C_ROPE_A = 0
C_ROPE_R = C_ROPE_A + 3 * 64
C_MASK = C_ROPE_R + 3 * 256
C_DECAY = C_MASK + 144 + 256
C_END = C_DECAY + RET_HEADS * 2 * TOK


def projection_groups():
    groups = [("aq", 0, 512, (0, 1)), ("aq", 512, 512, (0, 1)), ("akv", COL_AK, 256, (0, 1, 2))]
    width = RET_HEADS * RHD
    for pair in range(2):
        for n, kind in enumerate(("rq", "rk", "rv", "rg")):
            groups.append((kind, COL_RET + n * width + pair * 512, 512,
                           (0, 1) if kind in ("rq", "rg") else (0, 1, 2)))
    return groups


GROUPS = projection_groups()


def schedule():
    turn = lambda g: [("turn", g, b) for b in GROUPS[g][3]]
    rope = lambda g: [("rope", g, b) for b in GROUPS[g][3]]
    copy = lambda g: [("copy", g, b) for b in GROUPS[g][3]]
    att = [(g, t) for g in range(2) for t in range(TILES)]
    s = [("ln", "in"), ("proj", 0), ("ln", "meta")] + turn(0) + [("proj", 1)] + rope(0) + turn(1)
    s += [("proj", 2)] + rope(1) + turn(2) + copy(2) + [("proj", 3)] + rope(2) + turn(3)
    s += [("proj", 4)] + rope(3) + turn(4) + [("attS", *att[0])]
    s += [("proj", 5)] + copy(5) + rope(4) + [("attO", *att[0]), ("attS", *att[1])]
    s += [("proj", 6)] + copy(6) + [("retS", 0), ("attO", *att[1]), ("attS", *att[2]), ("retO", 0)]
    s += [("proj", 7)] + turn(7) + [("retS", 1), ("attO", *att[2]), ("retT", 0), ("attS", *att[3]), ("retO", 1)]
    s += [("proj", 8)] + rope(7) + turn(8) + [("attO", *att[3]), ("retT", 1)]
    s += [("proj", 9)] + rope(8) + copy(9) + [("retS", 2)]
    s += [("proj", 10)] + copy(10) + [("retO", 2)]
    s += [("out", 0, 0, 2), ("retS", 3), ("retT", 2), ("out", 0, 2, 4), ("retO", 3), ("out", 0, 4, LATE)]
    s += [("retT", 3), ("out", 0, LATE, LOADS)]
    s += [("out", g, 0, LOADS) for g in (1, 2, 3)] + [("ln", "mix")]
    for g in range(4):
        s += [("pq", g), ("subT", g)]
        if g:
            s += [("ps", 0, g - 1)]
        if g in (1, 2):
            s += [("pick", g - 1)]
    s += [("ps", 0, 3)] + [("ps", 1, b) for b in range(4)]
    return s


SCHED = schedule()


class Plan:

    def __init__(self):
        self.unit = {}
        self.readers = []
        self.t = {}
        self.d = {}
        self.stage = {}
        self.stage_t = []
        self.t_read = []
        counts = {"dve": 0, "act": 0}
        t_counts = {"dve": 0, "act": 0}
        self.t_split = {}
        nt = nd = 0

        def tile(key, engines):
            self.unit[key] = len(self.readers)
            self.readers.append(tuple(engines))

        for job in SCHED:
            kind = job[0]
            if kind == "proj":
                g = job[1]
                who = {"aq": ("dve",), "akv": ("dve", "act"), "rq": ("dve",), "rk": ("dve",),
                       "rv": ("act",), "rg": ("act",)}[GROUPS[g][0]]
                for b in GROUPS[g][3]:
                    tile(("proj", g, b), who)
            elif kind == "out" and job[2] == 0:
                for b in range(TILES):
                    tile(("out", job[1], b), ("dve",))
            elif kind == "pq":
                for b in range(4):
                    tile(("pq", job[1], b), ("act",))
            elif kind == "ps":
                tile(job, ("act",))
            n_t = {"ln": 1 if job[1] == "meta" else 4 * TILES, "rope": 1, "attO": 4, "retT": 1, "subT": 1}.get(kind, 0)
            self.t[job] = list(range(nt, nt + n_t))
            nt += n_t
            for t in self.t[job]:
                last = "dve" if kind in ("ln", "retT") else "act"
                if last == "dve":
                    self.t_split[t] = len(self.t_split)
                t_counts[last] += 1
                self.t_read.append((last, t_counts[last]))
            n_d = {"attS": 4, "attO": 1, "retS": 2, "retO": 1}.get(kind, 0)
            self.d[job] = list(range(nd, nd + n_d))
            nd += n_d
            if kind == "rope":
                self.stage[job] = self.stage[("turn", *job[1:])] = len(self.stage_t)
                self.stage_t.append(self.t[job][0])
        self.freed = []
        for who in self.readers:
            now = {}
            for e in who:
                counts[e] += 1
                now[e] = counts[e]
            self.freed.append(now)


PLAN = Plan()


def build(nc, x, meta, ln_in_g, ln_in_b, w_in, sinks, w_out, ln_mix_g, ln_mix_b, wq, subkeys,
          peer_u, peer_v, ln_ffn_g, ln_ffn_b, consts, ident_c, iota_c, out):
    with ExitStack() as ctx:
        sem = lambda name: ctx.enter_context(nc.semaphore(name))

        def at(name, shape, offset, dt=F32):
            return nc.alloc_sbuf_tensor_at(name, [P] + shape, dt, offset=offset)

        small = lambda name, shape, dt=F32: ctx.enter_context(nc.sbuf_tensor(name, [P] + shape, dt))
        ident = small("ident", [P])
        iota = small("iota", [P])
        stats = small("stats", [TILES, 4, 6])
        mv = small("mv", [TILES, 2])
        rstd = small("rstd", [2, TILES])
        ids = small("ids", [TILES, PICKS], U32)
        gates = small("gates", [TILES, PICKS])
        sink = small("sink", [AQ_HEADS])
        mx = small("mx", [4, 8])
        gn = small("gn", [2, TILES])
        gsum = small("gsum", [2, PH])
        lot = [small(f"lot{i}", [3, BANKS * GROUP]) for i in range(2)]
        idq = small("idq", [2, OCT], U32)

        KB = 1024
        r_stream = -(-nc.sbuf_base // 32) * 32
        r_hT = r_stream + 4 * (4 * TOK + 4 * KEYS + 5 * GCOLS)
        r_work = r_hT + 4 * KC * KEYS
        r_qT = r_work + 8 * KB
        r_rest = r_qT + 8 * KB
        r_hT_lo = r_rest
        r_mix = r_hT_lo + 4 * KC * KEYS
        r_raw = r_mix + 32 * KB
        r_split = r_raw + NRAW * QK * 4 * GCOLS
        r_tab = r_split + NSPLIT * 2 * QK * 4 * GCOLS
        r_misc = r_tab + 4 * (C_END + 2 * GCOLS)

        h = at("h", [TILES, D], r_stream)
        rqT = at("rqT", [4, TOK], r_stream)
        rkT = at("rkT", [4, KEYS], r_stream + 16 * TOK)
        rvg = at("rvg", [5, GCOLS], r_stream + 16 * TOK + 16 * KEYS)
        rv, rg = rvg[:, 0:3, :], rvg[:, 3:5, :]

        hT = at("hT", [KC, KEYS], r_hT, F32R)
        hT_lo = at("hT_lo", [KC, KEYS], r_hT_lo, F32R)
        mixT = at("mixT", [KC, TOK], r_mix, F32R)
        mixT_lo = at("mixT_lo", [KC, TOK], r_mix + 16 * KB, F32R)
        w_raw = at("w_raw", [NRAW, QK, GCOLS], r_raw)
        w_hi = at("w_hi", [NSPLIT, QK, GCOLS], r_split, F32R)
        w_lo = at("w_lo", [NSPLIT, QK, GCOLS], r_split + NSPLIT * QK * 4 * GCOLS, F32R)

        gb = at("gb", [2, D], r_tab)
        consts_sb = at("consts_sb", [C_END], r_tab)
        ropeA = at("ropeA", [GCOLS], r_tab + 4 * C_END)
        ropeB = at("ropeB", [GCOLS], r_tab + 4 * (C_END + GCOLS))

        xm_t = at("xm", [D], r_mix)
        xm = xm_t[0:META, :]
        pqT = at("pqT", [2 * PH, TOK], r_mix)
        skT = at("skT", [2 * PH, NKEY], r_mix + 16 * KB)
        subn = at("subn", [4, P], r_mix + 24 * KB)

        work = at("work", [8 * TOK], r_work)
        prob = work[:, :].rearrange("p (h k) -> p h k", h=8)
        qT = at("qT", [8, TOK], r_qT)
        stage = at("stage", [STAGES, GCOLS], r_misc)
        pT = at("pT", [2, 4, P], r_misc + 6 * KB)
        kT = at("kT", [2, KEYS], r_misc + 10 * KB)
        av = at("av", [3, P], r_misc + 10 * KB + 8 * KEYS)
        sT = at("sT", [5 * P], r_misc + 10 * KB + 8 * KEYS + 12 * P)
        gated = at("gated", [TILES, RHD], r_misc + 10 * KB + 8 * KEYS + 32 * P)

        r_tail = r_rest + 4 * NKEY * TOK
        grid = at("grid", [NKEY, TOK], r_rest)
        U = [at(f"U{i}", [D], r) for i, r in enumerate((r_tail, r_tail + 8 * KB, r_hT, r_hT + 8 * KB)
                                                      + (r_rest, r_rest + 8 * KB, r_raw + 16 * KB, r_raw + 24 * KB))]
        hot = [[at(f"hot{e}{i}", [2, PAIR, P], r + 2 * KB * i) for i in range(n)]
               for e, n, r in ((0, 2, r_tail + 16 * KB), (1, HOT_SLOTS, r_tail + 8 * KB))]
        turned = at("turned", [3, P], r_tail + 20 * KB)
        square = at("square", [2, 256], r_tail + 22 * KB)
        alphaI = at("alphaI", [P], r_tail + 20 * KB + 12 * P)
        halves = at("halves", [TILES, 2, PICKS], r_stream + 16 * KB)
        dots = at("dots", [TILES * PICKS], r_hT + 16 * KB)
        v_raw = [at(f"v_raw{i}", [D], r) for i, r in enumerate((r_work, r_qT, r_tail, r_tail + 8 * KB))]
        v_hi = [at(f"v_hi{i}", [D], r, F32R) for i, r in enumerate((r_hT, r_stream))]
        v_lo = [at(f"v_lo{i}", [D], r + 8 * KB, F32R) for i, r in enumerate((r_hT, r_stream))]
        g_hi = at("g_hi", [V_SPLIT, TOK], r_tail + 16 * KB, F32R)
        g_lo = at("g_lo", [V_SPLIT, TOK], r_tail + 18 * KB, F32R)
        gb_last = at("gb_last", [2, D], r_rest)
        result = at("result", [TILES, D], r_rest + 16 * KB)
        h_saved = nc.dram_tensor("h_saved", (TOK, D), F32, kind="Internal").ap()

        def psum(name, dt=F32):
            return ctx.enter_context(nc.psum_tensor(name, [P, 512], dt))

        pj = [psum(f"pj{i}") for i in range(4)]
        tb = [psum(f"tb{i}") for i in range(2)]
        db = [psum(f"db{i}") for i in range(2)]

        consts_in = sem("consts_in")
        x_in = [sem(f"x_in{i}") for i in range(3)]
        gb_in = sem("gb_in")
        gb_half_in = [sem(f"gb_half_in{i}") for i in range(2)]
        raw_in = [sem(f"raw_in{i}") for i in range(NRAW)]
        hi_done = sem("hi_done")
        lo_done = {"pool": sem("lo_done_pool"), "dve": sem("lo_done_dve")}
        w_used = sem("w_used")
        saved, back = sem("saved"), sem("back")
        tables_in = sem("tables_in")
        pj_full = sem("pj_full")
        pj_read = {"dve": sem("pj_read_dve"), "act": sem("pj_read_act")}
        t_full, t_hi = sem("t_full"), sem("t_hi")
        t_read = {"dve": sem("t_read_dve"), "act": sem("t_read_act")}
        d_full, d_read = sem("d_full"), sem("d_read")
        stage_full = sem("stage_full")
        dve_step = sem("dve_step")
        act_step = sem("act_step")
        norm_var, norm_sd = sem("norm_var"), sem("norm_sd")
        ln_part, ln_done = sem("ln_part"), sem("ln_done")
        soft_max, soft_exp, soft_prob = sem("soft_max"), sem("soft_exp"), sem("soft_prob")
        ret_gated = sem("ret_gated")
        keys_taken = sem("keys_taken")
        gvar, gsd = sem("gvar"), sem("gsd")
        picks_ready = sem("picks_ready")
        fexp_in, fexp_out = sem("fexp_in"), sem("fexp_out")

        def rope_tab(kind, b, n):
            half = AHD // 2 if kind[0] == "a" else RHD // 2
            o = (C_ROPE_A if kind[0] == "a" else C_ROPE_R) + b * 2 * half
            return consts_sb[0:n, o:o + half], consts_sb[0:n, o + half:o + 2 * half]

        mask = [consts_sb[:, C_MASK:C_MASK + 144], consts_sb[:, C_MASK + 144:C_MASK + 400]]
        decay = consts_sb[:, C_DECAY:C_END].rearrange("p (h m q) -> p h m q", h=RET_HEADS, m=2)
        rows = lambda b: META if b == 2 else P
        spots = {0: (0, P), 1: (P, TOK), 2: (TOK, KEYS)}
        keyspots = {2: (0, META), 0: (META, META + P), 1: (META + P, KEYS)}
        lo = [0, META]
        nkeys = [META + P, TOK]
        loads = [(w_in, c0, n, q) for _, c0, n, _ in GROUPS for q in range(LOADS)]
        loads += [(src, g * GCOLS, GCOLS, q) for src in (w_out, wq) for g in range(4) for q in range(LOADS)]
        first_out = len(GROUPS) * LOADS
        first_wq = first_out + 4 * LOADS
        last_unit = [PLAN.unit[("proj", g, GROUPS[g][3][-1])] for g in range(len(GROUPS))]
        last_unit += [PLAN.unit[(kind, g, b)] for kind, b in (("out", 1), ("pq", 3)) for g in range(4)]

        def wait_used(eng, n):
            group, q = divmod(n, LOADS)
            if q == LOADS - 1:
                eng.wait_ge(pj_full, last_unit[group] + 1)
            else:
                eng.wait_ge(w_used, group * (LOADS - 1) + q + 1)

        def lo_by(n):
            return "dve" if n >= first_out + 2 * LOADS - 2 else "pool"

        def wait_split(eng, n):
            eng.wait_ge(lo_done[lo_by(n)], sum(lo_by(m) == lo_by(n) for m in range(n + 1)))

        def split_rest(eng, n):
            cols = loads[n][2]
            eng.tensor_tensor(w_lo[:, n % NSPLIT, :, 0:cols], w_raw[:, n % NRAW, :, 0:cols],
                              w_hi[:, n % NSPLIT, :, 0:cols].bitcast(F32), ALU.subtract).then_inc(lo_done[lo_by(n)], 1)

        def wait_t_read(eng, t):
            last, count = PLAN.t_read[t]
            eng.wait_ge(t_read[last], count)

        sub_in_q = [sem(f"sub_in{i}") for i in range(4)]

        u_in = [sem(f"u_in{i}") for i in range(SLOTS[0])]
        u_free = sem("u_free")
        ids_staged = sem("ids_staged")
        slot_seen = sem("slot_seen")
        lot_taken = [sem(f"lot_taken{i}") for i in range(2)]
        gelus, weights, weights_t, turned_ready = sem("gelus"), sem("weights"), sem("weights_t"), sem("turned_ready")
        hot_full, hot_used = [sem(f"hot_full{i}") for i in range(2)], sem("hot_used")
        grid_read = sem("grid_read")
        alpha_ready, seeded = sem("alpha_ready"), sem("seeded")
        v_in = [sem(f"v_in{i}") for i in range(V_RAW)]
        g_rounded = sem("g_rounded")
        v_added = sem("v_added")
        v_rounded, v_split, v_used = sem("v_rounded"), sem("v_split"), sem("v_used")
        out_done = sem("out_done")
        acc = [tb + db, pj]

        by_key = lambda n: qT[:, n, :].rearrange("p (m k) -> p m k", m=16)
        sv, si, sif = by_key(0), by_key(1).bitcast(U32), by_key(2)
        fv = qT[:, 3, 0:PICKS].rearrange("p (m k) -> p m k", m=8)
        fi = qT[:, 3, PICKS:].bitcast(U32).rearrange("p (m k) -> p m k", m=8)
        by_half = lambda n: qT[:, n, :].rearrange("p (s m k) -> p s m k", s=2, m=8)
        fab, fabf = by_half(4).bitcast(U32), by_half(5)

        block = ctx.enter_context(nc.Block())

        @block.sync
        def _(sp):
            sp.dma_start(h[:, 0, :], x[0:P, :]).then_inc(x_in[0], 16)
            sp.dma_start(h[:, 1, :], x[P:TOK, :]).then_inc(x_in[1], 16)
            for half, cols in enumerate((slice(0, D // 2), slice(D // 2, D))):
                sp.dma_start(gb[:, 0, cols], ln_in_g[cols].partition_broadcast(P)).then_inc(gb_half_in[half], 16)
                sp.dma_start(gb[:, 1, cols], ln_in_b[cols].partition_broadcast(P)).then_inc(gb_half_in[half], 16)
            sp.dma_start(ident[:, :], ident_c).then_inc(consts_in, 16)
            sp.dma_start(xm, meta).then_inc(x_in[2], 16)
            sp.dma_start(iota[:, :], iota_c).then_inc(consts_in, 16)
            sp.dma_start(sink[:, :], sinks.partition_broadcast(P)).then_inc(consts_in, 16)
            for n, (src, c0, cols, q) in enumerate(loads):
                if n >= NRAW:
                    wait_split(sp, n - NRAW)
                sp.dma_start(w_raw[:, n % NRAW, :, 0:cols],
                             src[q * QK * P:(q + 1) * QK * P, c0:c0 + cols]
                             .rearrange("(k p) c -> p k c", p=P)).then_inc(raw_in[n % NRAW], 16)
                if n == NRAW + NSPLIT - 1:
                    sp.wait_ge(ln_part, 4 * TILES)
                    sp.wait_ge(ln_done, 1)
                    sp.dma_start(consts_sb[:, :], consts).then_inc(tables_in, 16)
                    for tile in range(TILES):
                        sp.dma_start(h_saved[tile * P:(tile + 1) * P, :], h[:, tile, :]).then_inc(saved, 16)
                if n == first_out + LATE + NSPLIT - 1:
                    sp.wait_ge(d_full, PLAN.d[("retO", 3)][0] + 1)
                    sp.wait_ge(ret_gated, 4)
                    sp.wait_ge(saved, 32)
                    for tile in range(TILES):
                        sp.dma_start(h[:, tile, :], h_saved[tile * P:(tile + 1) * P, :]).then_inc(back, 16)
                    sp.dma_start(gb[:, 0, :], ln_mix_g.partition_broadcast(P)).then_inc(gb_in, 16)
                    sp.dma_start(gb[:, 1, :], ln_mix_b.partition_broadcast(P)).then_inc(gb_in, 16)
                if n > first_wq and (n % LOADS == 0 or n == len(loads) - 1):
                    sub = (n - first_wq) // LOADS - (n % LOADS == 0)
                    if sub:
                        sp.wait_ge(t_full, PLAN.t[("subT", sub - 1)][0] + 1)
                    else:
                        sp.wait_ge(pj_full, PLAN.unit[("out", 3, 1)] + 1)
                    sp.dma_start(subn[:, :, :], subkeys[:, 4 * sub:4 * sub + 4, :]).then_inc(sub_in_q[sub], 16)

            def load_chunk(c, k):
                sp.dma_start(v_raw[k][:, :], peer_v[bass.ts(c, P), :]).then_inc(v_in[k], 16)

            for k in range(V_RAW):
                if k == 0:
                    sp.wait_ge(picks_ready, TILES * PARTS)
                if k == 2:
                    sp.wait_ge(u_free, SLOTS[0] + TILES * PICKS)
                if k == 3:
                    sp.wait_ge(hot_used, 2 + TILES * ROUNDS * FILLS)
                load_chunk(k, k)
            for first, end in ((1, 16), (16, NKEY // V_RAW)):
                with sp.Fori(first, end) as i:
                    for k in range(V_RAW):
                        sp.wait_ge(v_split, (i - 1) * V_RAW + k + 1)
                        load_chunk(i * V_RAW + k, k)
                if first == 1:
                    sp.wait_ge(v_split, 16)
                    sp.dma_start(gb_last[:, 0, :], ln_ffn_g.partition_broadcast(P)).then_inc(gb_in, 16)
                    sp.dma_start(gb_last[:, 1, :], ln_ffn_b.partition_broadcast(P)).then_inc(gb_in, 16)
            for tile in range(TILES):
                for half in range(2):
                    cols = slice(half * D // 2, (half + 1) * D // 2)
                    sp.wait_ge(ln_part, 4 * (2 * TILES + tile) + 2 * half + 2)
                    sp.dma_start(out[tile * P:(tile + 1) * P, cols], result[:, tile, cols]).then_inc(out_done, 16)
            sp.wait_ge(out_done, 32 * TILES)

        @block.tensor
        def _(pe):
            def unit_bank(u):
                if u >= 4:
                    for e, n in PLAN.freed[u - 4].items():
                        pe.wait_ge(pj_read[e], n)
                return pj[u % 4]

            def t_bank(t):
                if t >= 2:
                    wait_t_read(pe, t - 2)
                return tb[t % 2]

            def d_bank(d):
                if d >= 2:
                    pe.wait_ge(d_read, d - 1)
                return db[d % 2]

            def product(units, group, q0, q1, lhs, rows_of, cols, ready=None):
                for q in range(q0, q1):
                    n = group * LOADS + q
                    slot = n % NSPLIT
                    wait_split(pe, n)
                    if ready:
                        wait_t_read(pe, ready[q * QK // 4])
                    for b, u in units:
                        bank = (unit_bank(u) if q == 0 else pj[u % 4])[0:rows_of(b), 0:cols]
                        for k in range(QK):
                            kk = q * QK + k
                            hi, lo = lhs(b, kk)
                            wh, wl = w_hi[:, slot, k, 0:cols], w_lo[:, slot, k, 0:cols]
                            nc.tensor.matmul(bank, hi, wh, start=kk == 0, stop=False)
                            nc.tensor.matmul(bank, hi, wl, start=False, stop=False)
                            last = nc.tensor.matmul(bank, lo, wh, start=False, stop=kk == KC - 1)
                        if q == LOADS - 1:
                            last.then_inc(pj_full, 1)
                    if q < LOADS - 1:
                        last.then_inc(w_used, 1)

            for job in SCHED:
                kind = job[0]
                if kind == "ln" and job[1] == "meta":
                    pe.wait_ge(ln_done, 1)
                    bank = t_bank(PLAN.t[job][0])
                    for k in range(KC):
                        last = nc.tensor.matmul(bank[:, k * META:(k + 1) * META], xm[:, k * P:(k + 1) * P],
                                                ident[0:META, 0:META], start=True, stop=True)
                    last.then_inc(t_full, 1)
                elif kind == "ln":
                    if job[1] == "in":
                        pe.wait_ge(consts_in, 48)
                    for i, t in enumerate(PLAN.t[job]):
                        q, tile = divmod(i, TILES)
                        pe.wait_ge(ln_part, i + 1 + (4 * TILES if job[1] == "mix" else 0))
                        bank = t_bank(t)
                        for k in range(4):
                            kk = 4 * q + k
                            last = nc.tensor.transpose(bank[:, k * P:(k + 1) * P],
                                                       h[:, tile, kk * P:(kk + 1) * P], ident[:, :])
                        last.then_inc(t_full, 1)
                elif kind == "proj":
                    g = job[1]
                    if g == 2:
                        wait_t_read(pe, PLAN.t[("ln", "meta")][0])
                    product([(b, PLAN.unit[("proj", g, b)]) for b in GROUPS[g][3]], g, 0, LOADS,
                            lambda b, kk: [t[:, kk, spots[b][0]:spots[b][1]] for t in (hT, hT_lo)], rows, GROUPS[g][2],
                            PLAN.t[("ln", "in")][TILES - 1::TILES] if g == 0 else None)
                elif kind == "rope":
                    _, g, b = job
                    t = PLAN.t[job][0]
                    pe.wait_ge(stage_full, PLAN.stage[job] + 1)
                    bank = t_bank(t)
                    src = stage[:, PLAN.stage[job] % STAGES, :]
                    n = rows(b)
                    for c in range(2 if g == 2 else 4):
                        if b == 2:
                            last = nc.tensor.matmul(bank[:, c * META:(c + 1) * META], src[0:META, c * P:(c + 1) * P],
                                                    ident[0:META, 0:META], start=True, stop=True)
                        else:
                            last = nc.tensor.transpose(bank[:, c * P:(c + 1) * P], src[:, c * P:(c + 1) * P], ident[:, :])
                    last.then_inc(t_full, 1)
                elif kind == "attS":
                    _, g, tile = job
                    if (g, tile) == (0, 0):
                        wait_t_read(pe, PLAN.t[("rope", 2, 2)][0])
                    for i, d in enumerate(PLAN.d[job]):
                        bank = d_bank(d)
                        e = i % 2
                        for j in range(2):
                            last = nc.tensor.matmul(bank[:, j * nkeys[tile]:(j + 1) * nkeys[tile]],
                                                    qT[64 * e:64 * e + 64, 4 * g + 2 * (i // 2) + j, tile * P:(tile + 1) * P],
                                                    kT[64 * e:64 * e + 64, g, lo[tile]:lo[tile] + nkeys[tile]],
                                                    start=True, stop=True)
                        last.then_inc(d_full, 1)
                elif kind == "attO":
                    _, g, tile = job
                    n = 2 * g + tile
                    pe.wait_ge(soft_prob, n + 1)
                    n0 = META if tile == 0 else P
                    out_bank = None

                    def pv(pair):
                        wait_t_read(pe, PLAN.t[job][pair])
                        for e in range(2):
                            o = out_bank[64 * e:64 * e + 64, pair * P:(pair + 1) * P]
                            nc.tensor.matmul(o, av[0:n0, 2 if tile == 0 else 0, 64 * g:64 * g + 64],
                                             pT[0:n0, pair % 2, 2 * e, :], start=True, stop=False)
                            last = nc.tensor.matmul(o, av[:, tile, 64 * g:64 * g + 64],
                                                    pT[:, pair % 2, 2 * e + 1, :], start=False, stop=True)
                        return last

                    for pair, t in enumerate(PLAN.t[job]):
                        bank = t_bank(t)
                        for e in range(2):
                            src = prob[:, 2 * pair + e, :]
                            if tile == 0:
                                nc.tensor.matmul(bank[0:META, 2 * e * P:(2 * e + 1) * P], src[:, 0:META], ident[:, :],
                                                 start=True, stop=True)
                            else:
                                nc.tensor.transpose(bank[:, 2 * e * P:(2 * e + 1) * P], src[:, 0:P], ident[:, :])
                            last = nc.tensor.transpose(bank[:, (2 * e + 1) * P:(2 * e + 2) * P], src[:, n0:n0 + P], ident[:, :])
                        last.then_inc(t_full, 1)
                        if pair == 1:
                            out_bank = d_bank(PLAN.d[job][0])
                        if pair >= 1:
                            pv(pair - 1)
                    pv(3).then_inc(d_full, 1)
                elif kind == "retS":
                    hd = job[1]
                    c = 2 * (hd % 2)
                    d0, d1 = PLAN.d[job]
                    wait_t_read(pe, PLAN.t[("rope", 4 if hd < 2 else 8, 2)][0])
                    bank = d_bank(d0)
                    for k in range(2):
                        nc.tensor.matmul(bank[:, 0:TOK], rkT[:, c + k, META:META + P], rqT[:, c + k, :],
                                         start=k == 0, stop=k == 1)
                    for k in range(2):
                        last = nc.tensor.matmul(bank[:, TOK:TOK + P], rkT[:, c + k, META + P:KEYS], rqT[:, c + k, P:TOK],
                                                start=k == 0, stop=k == 1)
                    last.then_inc(d_full, 1)
                    bank = d_bank(d1)
                    for k in range(2):
                        last = nc.tensor.matmul(bank[0:META, 0:TOK], rkT[:, c + k, 0:META], rqT[:, c + k, :],
                                                start=k == 0, stop=k == 1)
                    last.then_inc(d_full, 1)
                elif kind == "retO":
                    hd = job[1]
                    pe.wait_ge(d_read, PLAN.d[("retS", hd)][1] + 1)
                    pe.wait_ge(pj_read["act"], PLAN.freed[PLAN.unit[("proj", 5 if hd < 2 else 9, 2)]]["act"])
                    bank = d_bank(PLAN.d[job][0])
                    v = lambda b: rv[0:rows(b), b, (hd % 2) * RHD:(hd % 2 + 1) * RHD]
                    nc.tensor.matmul(bank[:, 0:RHD], sT[0:META, 3 * P:4 * P], v(2), start=True, stop=False)
                    nc.tensor.matmul(bank[:, 0:RHD], sT[:, 0:P], v(0), start=False, stop=True)
                    nc.tensor.matmul(bank[:, RHD:2 * RHD], sT[0:META, 4 * P:5 * P], v(2), start=True, stop=False)
                    nc.tensor.matmul(bank[:, RHD:2 * RHD], sT[:, P:2 * P], v(0), start=False, stop=False)
                    nc.tensor.matmul(bank[:, RHD:2 * RHD], sT[:, 2 * P:3 * P], v(1), start=False,
                                     stop=True).then_inc(d_full, 1)
                elif kind == "retT":
                    hd = job[1]
                    pe.wait_ge(ret_gated, hd + 1)
                    bank = t_bank(PLAN.t[job][0])
                    for tile in range(TILES):
                        for c in range(2):
                            i = 2 * tile + c
                            last = nc.tensor.transpose(bank[:, i * P:(i + 1) * P], gated[:, tile, c * P:(c + 1) * P], ident[:, :])
                    last.then_inc(t_full, 1)
                elif kind == "subT":
                    q = job[1]
                    pe.wait_ge(sub_in_q[q], 16)
                    bank = t_bank(PLAN.t[job][0])
                    for c in range(4):
                        last = nc.tensor.transpose(bank[:, c * P:(c + 1) * P], subn[:, c, :], ident[:, :])
                    last.then_inc(t_full, 1)
                elif kind == "out":
                    _, g, q0, q1 = job
                    if g == 0:
                        wait_t_read(pe, PLAN.t[("retT", 3 if q0 == LATE else 1)][0])
                        pe.wait_ge(d_read, PLAN.d[("attO", 1, 1)][0] + 1)
                    product([(b, PLAN.unit[("out", g, b)]) for b in range(TILES)], len(GROUPS) + g, q0, q1,
                            lambda b, kk: [t[:, kk, b * P:(b + 1) * P] for t in (mixT, mixT_lo)], rows, GCOLS)
                elif kind == "pq":
                    g = job[1]
                    for q in range(LOADS):
                        n = (len(GROUPS) + 4 + g) * LOADS + q
                        slot = n % NSPLIT
                        wait_split(pe, n)
                        if g == 0:
                            wait_t_read(pe, PLAN.t[("ln", "mix")][TILES * (q * QK // 4) + 1])
                        for b in range(4):
                            u = PLAN.unit[("pq", g, b)]
                            bank = (unit_bank(u) if q == 0 else pj[u % 4])[:, 0:TOK]
                            for k in range(QK):
                                kk = q * QK + k
                                wh, wl = (t[:, slot, k, b * P:(b + 1) * P] for t in (w_hi, w_lo))
                                nc.tensor.matmul(bank, wh, hT[:, kk, 0:TOK], start=kk == 0, stop=False)
                                nc.tensor.matmul(bank, wh, hT_lo[:, kk, 0:TOK], start=False, stop=False)
                                last = nc.tensor.matmul(bank, wl, hT[:, kk, 0:TOK], start=False, stop=kk == KC - 1)
                            if q == LOADS - 1:
                                last.then_inc(pj_full, 1)
                        if q < LOADS - 1:
                            last.then_inc(w_used, 1)
                elif kind == "ps":
                    _, tile, b = job
                    if tile == 0:
                        pe.wait_ge(pj_read["act"], PLAN.freed[PLAN.unit[("pq", b, 3)]]["act"])
                        wait_t_read(pe, PLAN.t[("subT", b)][0])
                    bank = unit_bank(PLAN.unit[job])
                    for c in range(4):
                        m = 4 * b + c
                        last = nc.tensor.matmul(bank[:, c * P:(c + 1) * P], pqT[:, m, tile * P:(tile + 1) * P],
                                                skT[:, m, :], start=True, stop=True)
                    last.then_inc(pj_full, 1)

            pe.wait_ge(alpha_ready, 1)
            for e in ("act", "dve"):
                pe.wait_ge(t_read[e], max(n for last, n in PLAN.t_read if last == e))
            pe.wait_ge(d_read, sum(map(len, PLAN.d.values())))
            pe.wait_ge(pj_read["act"], PLAN.freed[-1]["act"])

            def seed(tile, c):
                return nc.tensor.matmul(acc[tile][c][:, :], alphaI[:, :], h[:, tile, c * 512:(c + 1) * 512],
                                        start=True, stop=False, skip_group_check=True)

            for tile in range(TILES):
                if tile == 1:
                    for c in (0, 2, 3):
                        seed(0, c)
                pe.wait_ge(weights, tile + 1)
                bank = acc[0][1]
                for s_, src in enumerate((halves[:, tile, 0, :], halves[:, tile, 1, :],
                                          dots[:, tile * PICKS:(tile + 1) * PICKS])):
                    last = nc.tensor.transpose(bank[:, s_ * P:(s_ + 1) * P], src, ident[:, :])
                last.then_inc(weights_t, 1)
                if tile == 1:
                    for c in range(GRID_BANKS, 4):
                        seed(1, c)
                    pe.wait_ge(turned_ready, TILES)
                    seed(0, 1)
                with pe.Fori(0, ROUNDS) as i:
                    r = i + tile * ROUNDS
                    for b in range(BANKS):
                        pe.wait_ge(grid_read, r * BANKS + b + 1)
                        bank = pj[b % GRID_BANKS]
                        for f in range(2):
                            g = 2 * b + f
                            if tile == 0:
                                pe.wait_ge(hot_full[0], i * FILLS + g + 1)
                                src = hot[0][f]
                            elif g in POOL_FILLS:
                                m = POOL_FILLS.index(g)
                                pe.wait_ge(hot_full[0], i * len(POOL_FILLS) + (ROUNDS * FILLS + m + 1))
                                src = hot[0][m]
                            else:
                                m = sum(x not in POOL_FILLS for x in range(g))
                                pe.wait_ge(hot_full[1], i * (FILLS - len(POOL_FILLS)) + m + 1)
                                src = hot[1][m % HOT_SLOTS]
                            for j in range(PAIR):
                                o = (PAIR * f + j) * P
                                last = nc.tensor.matmul(bank[:, o:o + P], src[:, 1, j, :], src[:, 0, j, :],
                                                        start=True, stop=True)
                            last.then_inc(hot_used, 1)
            pe.wait_ge(grid_read, GRID_BANKS + TILES * ROUNDS * BANKS)
            for c in range(GRID_BANKS):
                last = seed(1, c)
            last.then_inc(seeded, 1)

            def chunk(c, k):
                pe.wait_ge(v_split, c + 1)
                for tile in range(TILES):
                    cols = slice(tile * P, (tile + 1) * P)
                    for n in range(4):
                        d = slice(n * 512, (n + 1) * 512)
                        for g, v in ((g_hi, v_hi), (g_hi, v_lo), (g_lo, v_hi)):
                            last = nc.tensor.matmul(acc[tile][n][:, :], g[:, k, cols], v[k][:, d],
                                                    start=False, stop=False, skip_group_check=True)
                    last.then_inc(v_added if tile == 0 else v_used, 1)

            with pe.Fori(0, NKEY // V_SPLIT) as i:
                for k in range(V_SPLIT):
                    chunk(i * V_SPLIT + k, k)

        @block.scalar
        def _(act):
            steps = [0]

            def link(ins):
                steps[0] += 1
                ins.then_inc(act_step, 1)
                act.wait_ge(act_step, steps[0])

            def norm_sqrt(n):
                act.wait_ge(norm_var, n + 1)
                sd = rstd[:, 0, 0:NORM_TILES[n]]
                nc.scalar.activation(sd, sd, ACT.Sqrt).then_inc(norm_sd, 1)

            def gate_exp(tile):
                act.wait_ge(fexp_in, (tile + 1) * PARTS)
                nc.scalar.activation(gates[:, tile, :], gates[:, tile, :], ACT.Exp).then_inc(fexp_out, 1)

            rounded = [0]

            def round_weights(until):
                for n in range(rounded[0], min(until, len(loads))):
                    act.wait_ge(raw_in[n % NRAW], 16 * (n // NRAW + 1))
                    if n >= NSPLIT:
                        wait_used(act, n - NSPLIT)
                    cols = loads[n][2]
                    nc.scalar.copy(w_hi[:, n % NSPLIT, :, 0:cols], w_raw[:, n % NRAW, :, 0:cols]).then_inc(hi_done, 1)
                    rounded[0] = n + 1

            for job in SCHED:
                kind = job[0]
                if kind == "proj":
                    round_weights((job[1] + 1) * LOADS + NSPLIT)
                elif kind == "out":
                    round_weights((len(GROUPS) + job[1]) * LOADS + job[3] + NSPLIT)
                elif kind == "pq":
                    round_weights((len(GROUPS) + 4 + job[1] + 1) * LOADS + NSPLIT)
                if kind == "ln" and job[1] == "meta":
                    t = PLAN.t[job][0]
                    act.wait_ge(t_full, t + 1)
                    nc.scalar.copy(hT[:, :, TOK:KEYS],
                                   tb[t % 2][:, 0:KC * META].rearrange("p (k n) -> p k n", k=KC)).then_inc(t_hi, 1)
                elif kind == "ln":
                    norm_sqrt(0 if job[1] == "in" else 2)
                    if job[1] == "mix":
                        act.wait_ge(pj_full, PLAN.unit[("proj", 10, 1)] + 1)
                    for i, t in enumerate(PLAN.t[job]):
                        q, tile = divmod(i, TILES)
                        act.wait_ge(t_full, t + 1)
                        nc.scalar.copy(hT[:, 4 * q:4 * q + 4, spots[tile][0]:spots[tile][1]],
                                       tb[t % 2][:, :].rearrange("p (k n) -> p k n", k=4)).then_inc(t_hi, 1)
                        if tile == 1 and job[1] == "in":
                            round_weights(min(2 * q, NRAW))
                    if job[1] == "in":
                        norm_sqrt(1)
                elif kind == "rope":
                    _, g, b = job
                    t = PLAN.t[job][0]
                    gk = GROUPS[g][0]
                    if gk == "rq" and g == 3 and b == 0:
                        act.wait_ge(saved, 32)
                    if gk == "rq" and g == 7 and b == 0:
                        act.wait_ge(d_full, PLAN.d[("retS", 1)][1] + 1)
                    act.wait_ge(t_full, t + 1)
                    n = rows(b)
                    nch = 2 if gk == "akv" else 4
                    src = tb[t % 2][:, 0:nch * n].rearrange("p (c n) -> p c n", c=nch)
                    k0, k1 = keyspots[b]
                    dst = {"aq": lambda: qT[:, 4 * g:4 * g + 4, b * P:(b + 1) * P],
                           "akv": lambda: kT[:, :, k0:k1],
                           "rq": lambda: rqT[:, :, b * P:(b + 1) * P],
                           "rk": lambda: rkT[:, :, k0:k1]}[gk]()
                    nc.scalar.copy(dst, src).then_inc(t_read["act"], 1)
                elif kind == "copy":
                    _, g, b = job
                    u = PLAN.unit[("proj", g, b)]
                    act.wait_ge(pj_full, u + 1)
                    if g == 9 and b == 0:
                        act.wait_ge(d_full, PLAN.d[("retO", 1)][0] + 1)
                    if g == 10 and b == 0:
                        act.wait_ge(ret_gated, 2)
                    n = rows(b)
                    if GROUPS[g][0] == "akv":
                        act.wait_ge(pj_read["dve"], PLAN.freed[u]["dve"])
                        nc.scalar.copy(av[0:n, b, :], pj[u % 4][0:n, P:2 * P]).then_inc(pj_read["act"], 1)
                    elif GROUPS[g][0] == "rv":
                        nc.scalar.copy(rv[0:n, b, :], pj[u % 4][0:n, :]).then_inc(pj_read["act"], 1)
                    else:
                        nc.scalar.activation(rg[:, b, :], pj[u % 4][:, :], ACT.Silu).then_inc(pj_read["act"], 1)
                elif kind == "attS":
                    _, g, tile = job
                    n = 2 * g + tile
                    act.wait_ge(soft_max, n + 1)
                    for e in range(8):
                        nc.scalar.activation(prob[:, e, 0:nkeys[tile]], prob[:, e, 0:nkeys[tile]], ACT.Exp,
                                             bias=mx[:, 0, e:e + 1], accum_out=mx[:, 2, e:e + 1])
                    nc.scalar.activation(mx[:, 1, :], mx[:, 1, :], ACT.Exp).then_inc(soft_exp, 1)
                elif kind == "attO":
                    _, g, tile = job
                    n0 = META if tile == 0 else P
                    for pair, t in enumerate(PLAN.t[job]):
                        act.wait_ge(t_full, t + 1)
                        src = tb[t % 2][:, :].rearrange("p (e k n) -> p e k n", e=2, k=2)
                        dst = pT[:, pair % 2, :, :].rearrange("p (e k) n -> p e k n", e=2)
                        if tile == 0:
                            nc.scalar.copy(dst[0:META, :, 0, :], src[0:META, :, 0, :])
                            nc.scalar.copy(dst[:, :, 1, :], src[:, :, 1, :]).then_inc(t_read["act"], 1)
                        else:
                            nc.scalar.copy(dst, src).then_inc(t_read["act"], 1)
                elif kind == "retO":
                    act.wait_ge(gvar, job[1] + 1)
                    nc.scalar.activation(gn[:, 1, :], gn[:, 1, :], ACT.Sqrt).then_inc(gsd, 1)
                elif kind == "retT":
                    hd = job[1]
                    t = PLAN.t[job][0]
                    act.wait_ge(t_full, t + 1)
                    c0 = 8 + 2 * hd
                    nc.scalar.copy(mixT[:, c0:c0 + 2, :].rearrange("p c (t n) -> p t c n", t=2),
                                   tb[t % 2][:, :].rearrange("p (t c n) -> p t c n", t=2, c=2)).then_inc(t_hi, 1)
                elif kind == "subT":
                    t = PLAN.t[job][0]
                    act.wait_ge(t_full, t + 1)
                    nc.scalar.copy(skT[:, 4 * job[1]:4 * job[1] + 4, :],
                                   tb[t % 2][:, :].rearrange("p (c n) -> p c n", c=4)).then_inc(t_read["act"], 1)
                elif kind == "pq":
                    for b in range(4):
                        u = PLAN.unit[("pq", job[1], b)]
                        act.wait_ge(pj_full, u + 1)
                        nc.scalar.copy(pqT[:, 4 * job[1] + b, :], pj[u % 4][:, 0:TOK]).then_inc(pj_read["act"], 1)
                elif kind == "ps":
                    _, tile, b = job
                    if (tile, b) == (1, 0):
                        act.wait_ge(keys_taken, PARTS)
                    u = PLAN.unit[job]
                    act.wait_ge(pj_full, u + 1)
                    nc.scalar.copy(work[:, b * 512:(b + 1) * 512], pj[u % 4][:, :]).then_inc(pj_read["act"], 1)

            def turn_over(tile):
                act.wait_ge(u_free, SLOTS[0] + (tile + 1) * PICKS)
                d = dots[:, tile * PICKS:(tile + 1) * PICKS]
                nc.scalar.activation(d, d, ACT.Gelu).then_inc(gelus, 1)
                act.wait_ge(weights_t, tile + 1)
                nc.scalar.copy(turned[:, :, :], acc[0][1][:, 0:3 * P].rearrange("p (s t) -> p s t", s=3)
                               ).then_inc(turned_ready, 1)

            def copy_grids(r, tile, first):
                for b in range(BANKS):
                    act.wait_ge(hot_used, 2 + r * FILLS + 2 * b + 2)
                    nc.scalar.copy(grid[:, :, bass.ds(first + b * GROUP, GROUP)].rearrange("p a t -> p t a"),
                                   pj[b % GRID_BANKS][:, :].rearrange("p (t a) -> p t a", t=GROUP)).then_inc(grid_read, 1)

            gate_exp(0)
            turn_over(0)
            for r in range(ROUNDS):
                if r == ROUNDS - 2:
                    gate_exp(1)
                copy_grids(r, 0, r * BANKS * GROUP)
            def round_rows(k, loaded, used=None):
                act.wait_ge(v_in[k], loaded * 16)
                if used is not None:
                    act.wait_ge(v_used, used)
                nc.scalar.copy(v_hi[k % V_SPLIT][:, :], v_raw[k][:, :]).then_inc(v_rounded, 1)

            def round_grid(c, k):
                nc.scalar.copy(g_hi[:, k % V_SPLIT, :], grid[:, bass.ds(c, 1), :].rearrange("p a t -> p (a t)")
                               ).then_inc(g_rounded, 1)

            turn_over(1)
            round_rows(0, 1)
            with act.Fori(0, ROUNDS) as i:
                copy_grids(i + ROUNDS, 1, i * (BANKS * GROUP) + P)
            act.wait_ge(grid_read, GRID_BANKS + TILES * ROUNDS * BANKS)
            round_grid(0, 0)
            for k in range(1, V_RAW):
                if k == 1:
                    act.wait_ge(seeded, 1)
                round_rows(k, 1, k - 1 if k >= V_SPLIT else None)
                round_grid(k, k)
            with act.Fori(1, NKEY // V_RAW) as i:
                for k in range(V_RAW):
                    round_rows(k, i + 1, i * V_RAW + (k - 1))
                    round_grid(i * V_RAW + k, k)
            norm_sqrt(3)

        dve_steps = [0]

        def link(ins):
            dve_steps[0] += 1
            ins.then_inc(dve_step, 1)
            nc.vector.wait_ge(dve_step, dve_steps[0])

        def take_lot(eng, lot_, taken, r, i):
            eng.tensor_copy(lot_[:, :, :], turned[:, :, bass.ts(i, BANKS * GROUP)]).then_inc(taken, 1)
            eng.wait_ge(taken, r + 1)

        def fill_hot(eng, lot_, rows_, f, tokens, done):
            for j in tokens:
                one = lambda s: lot_[:, s, f * PAIR + j:f * PAIR + j + 1]
                eng.tensor_scalar(rows_[:, 0, j, :], iota[:, :], one(0), None, ALU.is_equal)
                last = eng.tensor_scalar(rows_[:, 1, j, :], iota[:, :], one(1), one(2), ALU.is_equal, ALU.mult)
            if tokens[-1] == PAIR - 1:
                last.then_inc(done, 1)

        def norm_rows(number, n=P):
            tiles = slice(0, NORM_TILES[number])
            for tile in range(NORM_TILES[number]):
                last = nc.vector.bn_aggr(mv[0:n, tile, :], stats[0:n, tile, :, :].rearrange("p a b -> p (a b)"))
            link(last)
            if n < P:
                link(nc.vector.memset(rstd[:, 0, tiles], 1.0))
            nc.vector.tensor_scalar_add(rstd[0:n, 0, tiles], mv[0:n, tiles, 1], LN_EPS).then_inc(norm_var, 1)
            nc.vector.wait_ge(norm_sd, number + 1)
            link(nc.vector.reciprocal(rstd[0:n, 1, tiles], rstd[0:n, 0, tiles]))

        def norm_columns(parts, gain_bias, done):
            for dst, src, n, tile, cols in parts:
                last = nc.vector.scalar_tensor_tensor(out=dst, in0=src, scalar=mv[0:n, tile, 0:1],
                                                      in1=gain_bias[0:n, 0, cols], op0=ALU.subtract, op1=ALU.mult)
            link(last)
            for dst, src, n, tile, cols in parts:
                nc.vector.scalar_tensor_tensor(out=dst, in0=dst, scalar=rstd[0:n, 1, tile:tile + 1],
                                               in1=gain_bias[0:n, 1, cols], op0=ALU.mult, op1=ALU.add).then_inc(done, 1)

        @block.vector
        def _(dve):
            def best_keys(tile, part):
                dve.wait_ge(pj_read["act"], PLAN.freed[PLAN.unit[("ps", tile, part // 2)]]["act"])
                s3 = work[:, :].rearrange("p (m n) -> p m n", m=16)
                ms = (2 * part, 2 * part + 1)
                rest = [square[:, s, 0:NKEY] for s in range(2)]

                def step(f):
                    for s, m in enumerate(ms):
                        last = f(s, m)
                    link(last)

                step(lambda s, m: nc.vector.max(sv[:, m, 0:8], s3[:, m, :]))
                step(lambda s, m: nc.vector.max_index(si[:, m, 0:8], sv[:, m, 0:8], s3[:, m, :]))
                step(lambda s, m: nc.vector.match_replace(rest[s], sv[:, m, 0:8], s3[:, m, :], -3e38))
                step(lambda s, m: nc.vector.max(sv[:, m, 8:16], rest[s]))
                step(lambda s, m: nc.vector.max_index(si[:, m, 8:16], sv[:, m, 8:16], rest[s]))
                both = slice(2 * part, 2 * part + 2)
                nc.vector.tensor_copy(sif[:, both, :], si[:, both, :]).then_inc(keys_taken, 1)

            def picks(tile, part):
                dve.wait_ge(keys_taken, tile * PARTS + part + 1)
                m, m0 = part, 2 * part
                a, b = sv[:, m0, :], sv[:, m0 + 1, :]
                cand, rest = square[:, 0, :], square[:, 1, :]
                link(nc.vector.tensor_tensor(cand.rearrange("p (a b) -> p a b", a=16),
                                             a.unsqueeze(2).to_broadcast([P, 16, 16]),
                                             b.unsqueeze(1).to_broadcast([P, 16, 16]), ALU.add))
                best, where = fv[:, m, :], fi[:, m, :]
                link(nc.vector.max(best[:, 0:8], cand))
                nc.vector.max_index(where[:, 0:8], best[:, 0:8], cand)
                link(nc.vector.match_replace(rest, best[:, 0:8], cand, -3e38))
                link(nc.vector.max(best[:, 8:16], rest))
                link(nc.vector.max_index(where[:, 8:16], best[:, 8:16], rest))
                nc.vector.tensor_tensor(by_pick(gates[:, tile, :])[:, m, :], best, best[:, 0:1].to_broadcast([P, TOPK]),
                                        ALU.subtract).then_inc(fexp_in, 1)
                nc.vector.tensor_single_scalar(fab[:, 0, m, :], where, 4, ALU.logical_shift_right)
                link(nc.vector.tensor_single_scalar(fab[:, 1, m, :], where, 15, ALU.bitwise_and))
                link(nc.vector.tensor_copy(fabf[:, :, m, :], fab[:, :, m, :]))
                every = [P, 2, 16, 16]
                e = square[:, :, :].rearrange("p s (k r) -> p s k r", k=TOPK)
                link(nc.vector.tensor_tensor(e, fabf[:, :, m, :].unsqueeze(3).to_broadcast(every),
                                             iota[:, 0:TOPK].unsqueeze(1).unsqueeze(1).to_broadcast(every), ALU.is_equal))
                link(nc.vector.tensor_tensor(e, e, sif[:, m0:m0 + 2, :].unsqueeze(2).to_broadcast(every), ALU.mult))
                sub = halves[:, tile, :, m * TOPK:(m + 1) * TOPK]
                link(nc.vector.reduce_sum(sub, e, AX.X))
                nc.vector.scalar_tensor_tensor(out=by_pick(ids[:, tile, :])[:, m, :], in0=sub[:, 0, :],
                                               scalar=float(NKEY), in1=sub[:, 1, :],
                                               op0=ALU.mult, op1=ALU.add).then_inc(picks_ready, 1)

            by_pick = lambda t: t.rearrange("p (m k) -> p m k", m=PH)

            def norm_gates(tile):
                dve.wait_ge(fexp_out, tile + 1)
                gv = by_pick(gates[:, tile, :])
                link(nc.vector.reduce_sum(gsum[:, 0, :], gv, AX.X))
                link(nc.vector.reciprocal(gsum[:, 1, :], gsum[:, 0, :]))
                link(nc.vector.tensor_tensor(gv, gv, gsum[:, 1, :].unsqueeze(2).to_broadcast([P, PH, TOPK]), ALU.mult))

            def rope(src, heads, half, cos, sin, n):
                r = lambda a: a[0:n, 0:heads * 2 * half].rearrange("p (a s c) -> p a s c", a=heads, s=2)
                bc = lambda tab: tab.unsqueeze(1).unsqueeze(1).to_broadcast([n, heads, 2, half])
                a, b = r(ropeA), r(ropeB)
                s4 = src.rearrange("p (a s c) -> p a s c", a=heads, s=2)
                nc.vector.tensor_tensor(a, s4, bc(cos), ALU.mult)
                ins = nc.vector.tensor_tensor(b, s4, bc(sin), ALU.mult)
                ins.then_inc(pj_read["dve"], 1)
                return a, b

            def ln_rest(t, part, src):
                dve.wait_ge(t_hi, PLAN.t_split[t] + 1)
                nc.vector.tensor_tensor(hT_lo[part], src, hT[part].bitcast(F32), ALU.subtract).then_inc(t_read["dve"], 1)

            split = [0]

            def split_weights(until):
                for n in range(split[0], min(until, len(loads))):
                    if lo_by(n) == "dve":
                        dve.wait_ge(hi_done, n + 1)
                        split_rest(nc.vector, n)
                    split[0] = n + 1

            for job in SCHED:
                kind = job[0]
                if kind == "out":
                    split_weights((len(GROUPS) + job[1]) * LOADS + job[3] + NSPLIT)
                elif kind == "pq":
                    split_weights((len(GROUPS) + 4 + job[1] + 1) * LOADS + NSPLIT)
                if kind == "ln" and job[1] == "meta":
                    t = PLAN.t[job][0]
                    part = (slice(None), slice(None), slice(TOK, KEYS))
                    ln_rest(t, part, tb[t % 2][:, 0:KC * META].rearrange("p (k n) -> p k n", k=KC))
                elif kind == "ln":
                    if job[1] == "in":
                        for tile in range(TILES):
                            dve.wait_ge(x_in[tile], 16)
                            for c in range(4):
                                last = nc.vector.bn_stats(stats[:, tile, c, :], h[:, tile, c * 512:(c + 1) * 512])
                        link(last)
                        norm_rows(0)
                    else:
                        norm_rows(2)
                        dve.wait_ge(gb_in, 32)

                    def rests(q):
                        for tile in range(TILES):
                            t = PLAN.t[job][TILES * q + tile]
                            part = (slice(None), slice(4 * q, 4 * q + 4), slice(*spots[tile]))
                            ln_rest(t, part, tb[t % 2][:, :].rearrange("p (k n) -> p k n", k=4))

                    for q in range(4):
                        cols = slice(512 * q, 512 * q + 512)
                        if job[1] == "in" and q % 2 == 0:
                            dve.wait_ge(gb_half_in[q // 2], 32)
                        norm_columns([(h[:, tile, cols], h[:, tile, cols], P, tile, cols) for tile in range(TILES)],
                                     gb, ln_part)
                        if q:
                            rests(q - 1)
                    rests(3)
                    if job[1] == "in":
                        dve.wait_ge(x_in[2], 16)
                        for c in range(4):
                            last = nc.vector.bn_stats(stats[0:META, 0, c, :], xm[:, c * 512:(c + 1) * 512])
                        link(last)
                        norm_rows(1, META)
                        norm_columns([(xm, xm, META, 0, slice(None))], gb, ln_done)
                elif kind == "retT":
                    t = PLAN.t[job][0]
                    part = (slice(None), slice(8 + 2 * job[1], 10 + 2 * job[1]), slice(None))
                    dve.wait_ge(t_hi, PLAN.t_split[t] + 1)
                    nc.vector.tensor_tensor(mixT_lo[part].rearrange("p c (t n) -> p t c n", t=2),
                                            tb[t % 2][:, :].rearrange("p (t c n) -> p t c n", t=2, c=2),
                                            mixT[part].bitcast(F32).rearrange("p c (t n) -> p t c n", t=2),
                                            ALU.subtract).then_inc(t_read["dve"], 1)
                elif kind == "turn":
                    _, g, b = job
                    gk = GROUPS[g][0]
                    u = PLAN.unit[("proj", g, b)]
                    n = rows(b)
                    half = AHD // 2 if gk[0] == "a" else RHD // 2
                    heads = {"aq": 8, "akv": 2, "rq": 2, "rk": 2}[gk]
                    cos, sin = rope_tab(gk, b, n)
                    if g == 0 and b == 0:
                        dve.wait_ge(tables_in, 16)
                    dve.wait_ge(pj_full, u + 1)
                    a, bb = rope(pj[u % 4][0:n, 0:heads * 2 * half], heads, half, cos, sin, n)
                    dve.wait_ge(pj_read["dve"], PLAN.freed[u]["dve"])
                    s = PLAN.stage[job]
                    if s >= STAGES:
                        dve.wait_ge(t_full, PLAN.stage_t[s - STAGES] + 1)
                    st = stage[0:n, s % STAGES, :]
                    if gk == "akv":
                        o = st[:, 0:2 * P].rearrange("p (a t s c) -> p a t s c", a=2, t=2, s=2)
                        for copy in range(2):
                            nc.vector.tensor_tensor(o[:, :, copy, 0, :], a[:, :, 0, :], bb[:, :, 1, :], ALU.subtract)
                            last = nc.vector.tensor_tensor(o[:, :, copy, 1, :], a[:, :, 1, :], bb[:, :, 0, :], ALU.add)
                    else:
                        o = st.rearrange("p (a s c) -> p a s c", a=heads, s=2)
                        nc.vector.tensor_tensor(o[:, :, 0, :], a[:, :, 0, :], bb[:, :, 1, :], ALU.subtract)
                        last = nc.vector.tensor_tensor(o[:, :, 1, :], a[:, :, 1, :], bb[:, :, 0, :], ALU.add)
                    last.then_inc(stage_full, 1)
                    dve.wait_ge(stage_full, s + 1)
                elif kind == "attS":
                    _, g, tile = job
                    n = 2 * g + tile
                    nk = nkeys[tile]
                    if n == 0:
                        dve.wait_ge(consts_in, 48)
                    if n:
                        before = ("attO", (n - 1) // 2, (n - 1) % 2)
                        dve.wait_ge(t_full, PLAN.t[before][3] + 1)
                    for i, d in enumerate(PLAN.d[job]):
                        dve.wait_ge(d_full, d + 1)
                        h0 = 4 * (i // 2) + i % 2
                        nc.vector.scalar_tensor_tensor(
                            out=prob[:, h0:h0 + 3:2, 0:nk],
                            in0=db[d % 2][:, 0:2 * nk].rearrange("p (e k) -> p e k", e=2), scalar=AHD ** -0.5,
                            in1=mask[tile].unsqueeze(1).to_broadcast([P, 2, nk]),
                            op0=ALU.mult, op1=ALU.add).then_inc(d_read, 1)
                    dve.wait_ge(d_read, PLAN.d[job][3] + 1)
                    link(nc.vector.reduce_max(mx[:, 1, :], prob[:, :, 0:nk], AX.X))
                    sk = sink[:, 8 * g:8 * g + 8]
                    link(nc.vector.tensor_tensor(mx[:, 1, :], mx[:, 1, :], sk, ALU.max))
                    link(nc.vector.tensor_scalar_mul(mx[:, 0, :], mx[:, 1, :], -1.0))
                    nc.vector.tensor_tensor(mx[:, 1, :], sk, mx[:, 0, :], ALU.add).then_inc(soft_max, 1)
                    dve.wait_ge(soft_exp, n + 1)
                    link(nc.vector.tensor_tensor(mx[:, 2, :], mx[:, 2, :], mx[:, 1, :], ALU.add))
                    link(nc.vector.reciprocal(mx[:, 2, :], mx[:, 2, :]))
                    nc.vector.tensor_tensor(prob[:, :, 0:nk], prob[:, :, 0:nk],
                                            mx[:, 2, :].unsqueeze(2).to_broadcast([P, 8, nk]),
                                            ALU.mult).then_inc(soft_prob, 1)
                elif kind == "attO":
                    _, g, tile = job
                    d = PLAN.d[job][0]
                    dve.wait_ge(d_full, d + 1)
                    part = (slice(None), slice(4 * g, 4 * g + 4), slice(tile * P, (tile + 1) * P))
                    src = db[d % 2][:, :].rearrange("p (c n) -> p c n", c=4)
                    link(nc.vector.tensor_copy(mixT[part], src))
                    nc.vector.tensor_tensor(mixT_lo[part], src, mixT[part].bitcast(F32),
                                            ALU.subtract).then_inc(d_read, 1)
                elif kind == "retS":
                    hd = job[1]
                    d0, d1 = PLAN.d[job]
                    if hd:
                        dve.wait_ge(d_full, PLAN.d[("retO", hd - 1)][0] + 1)
                    dve.wait_ge(d_full, d0 + 1)
                    nc.vector.tensor_tensor(sT[:, 0:TOK], db[d0 % 2][:, 0:TOK], decay[:, hd, 0, :], ALU.mult)
                    nc.vector.tensor_tensor(sT[:, TOK:TOK + P], db[d0 % 2][:, TOK:TOK + P], decay[:, hd, 0, 0:P],
                                            ALU.mult).then_inc(d_read, 1)
                    dve.wait_ge(d_full, d1 + 1)
                    nc.vector.tensor_tensor(sT[0:META, 3 * P:5 * P], db[d1 % 2][0:META, 0:TOK], decay[0:META, hd, 1, :],
                                            ALU.mult).then_inc(d_read, 1)
                elif kind == "retO":
                    hd = job[1]
                    d = PLAN.d[job][0]
                    dve.wait_ge(d_full, d + 1)
                    if hd:
                        dve.wait_ge(t_full, PLAN.t[("retT", hd - 1)][0] + 1)
                    bank = db[d % 2][:, :].rearrange("p (t e) -> p t e", t=2)
                    for tile in range(TILES):
                        link(nc.vector.bn_stats(stats[:, 0, 0, :], bank[:, tile, :]))
                        link(nc.vector.bn_aggr(mv[:, 0, :], stats[:, 0, 0, :]))
                        link(nc.vector.tensor_copy(gn[:, 0, tile:tile + 1], mv[:, 0, 0:1]))
                        last = nc.vector.tensor_scalar_add(gn[:, 1, tile:tile + 1], mv[:, 0, 1:2], LN_EPS)
                        if tile == 0:
                            link(last)
                    last.then_inc(gvar, 1)
                    dve.wait_ge(gsd, hd + 1)
                    link(nc.vector.reciprocal(gn[:, 1, :], gn[:, 1, :]))
                    for tile in range(TILES):
                        last = nc.vector.tensor_scalar(gated[:, tile, :], bank[:, tile, :], gn[:, 0, tile:tile + 1],
                                                       gn[:, 1, tile:tile + 1], ALU.subtract, ALU.mult)
                    last.then_inc(d_read, 1)
                    dve.wait_ge(d_read, d + 1)
                    dve.wait_ge(pj_read["act"], PLAN.freed[PLAN.unit[("proj", 6 if hd < 2 else 10, 1)]]["act"])
                    nc.vector.tensor_tensor(gated[:, :, :], gated[:, :, :],
                                            rg[:, :, (hd % 2) * RHD:(hd % 2 + 1) * RHD], ALU.mult).then_inc(ret_gated, 1)
                elif kind == "out" and job[3] == LOADS:
                    g = job[1]
                    if g == 0:
                        dve.wait_ge(back, 32)
                    for b in range(TILES):
                        u = PLAN.unit[("out", g, b)]
                        dve.wait_ge(pj_full, u + 1)
                        hs = h[:, b, g * GCOLS:(g + 1) * GCOLS]
                        nc.vector.scalar_tensor_tensor(out=hs, in0=hs, scalar=ALPHA, in1=pj[u % 4][:, :],
                                                       op0=ALU.mult, op1=ALU.add).then_inc(pj_read["dve"], 1)
                        dve.wait_ge(pj_read["dve"], PLAN.freed[u]["dve"])
                        link(nc.vector.bn_stats(stats[:, b, g, :], hs))
                elif kind == "pick":
                    best_keys(0, job[1])
                    picks(0, job[1])

            dve.wait_ge(pj_full, PLAN.unit[("pq", 3, 3)] + 1)
            nc.vector.tensor_scalar_mul(alphaI[:, :], ident[:, :], ALPHA).then_inc(alpha_ready, 1)
            for j in range(TILES * PARTS):
                tile = j // PARTS
                after = divmod(j + 2, PARTS) if j + 2 < TILES * PARTS else None
                for turn in range(TURNS):
                    for n in range((j * TURNS + turn) * OCT, (j * TURNS + turn + 1) * OCT):
                        slot = n % SLOTS[tile]
                        row = U[slot][:, :]
                        before = tile * (PICKS // SLOTS[0])
                        dve.wait_ge(u_in[slot], (before + (n - tile * PICKS) // SLOTS[tile] + 1) * 16)
                        nc.vector.tensor_tensor_reduce(out=row, in0=row, in1=h[:, tile, :], scale=1.0,
                                                       scalar=0.0, op0=ALU.mult, op1=ALU.add,
                                                       accum_out=dots[:, n:n + 1]).then_inc(u_free, 1)
                    if turn == 0 and after:
                        best_keys(*after)
                if j % PARTS == PARTS - 2:
                    norm_gates(tile)
                if j % PARTS == PARTS - 1:
                    dve.wait_ge(gelus, tile + 1)
                    d = dots[:, tile * PICKS:(tile + 1) * PICKS]
                    nc.vector.tensor_tensor(d, d, gates[:, tile, :], ALU.mult).then_inc(weights, 1)
                if after:
                    picks(*after)
            dve.wait_ge(turned_ready, 2)
            mine = [f for f in range(FILLS) if f not in POOL_FILLS]
            with dve.Fori(0, ROUNDS) as i:
                take_lot(nc.vector, lot[1], lot_taken[1], i, i)
                for m, f in enumerate(mine):
                    last = max(x for x in range(len(mine)) if x % HOT_SLOTS == m % HOT_SLOTS)
                    before = mine[m - HOT_SLOTS] if m >= HOT_SLOTS else mine[last] - FILLS
                    dve.wait_ge(hot_used, i * FILLS + (2 + ROUNDS * FILLS + before + 1))
                    fill_hot(nc.vector, lot[1], hot[1][m % HOT_SLOTS], f, range(PAIR), hot_full[1])
                dve.wait_ge(hot_full[1], (i + 1) * len(mine))

            def split_chunk(c, k):
                dve.wait_ge(v_rounded, c + 1)
                nc.vector.tensor_tensor(v_lo[k % V_SPLIT][:, :], v_raw[k][:, :], v_hi[k % V_SPLIT][:, :].bitcast(F32),
                                        ALU.subtract)
                dve.wait_ge(g_rounded, c + 1)
                nc.vector.tensor_tensor(g_lo[:, k % V_SPLIT, :], grid[:, bass.ds(c, 1), :].rearrange("p a t -> p (a t)"),
                                        g_hi[:, k % V_SPLIT, :].bitcast(F32), ALU.subtract).then_inc(v_split, 1)

            with dve.Fori(0, NKEY // V_RAW) as i:
                for k in range(V_RAW):
                    split_chunk(i * V_RAW + k, k)
            for tile in range(TILES):
                dve.wait_ge((v_added, v_used)[tile], NKEY)
                for c in range(4):
                    last = nc.vector.bn_stats(stats[:, tile, c, :], acc[tile][c][:, :])
            link(last)
            norm_rows(3)
            dve.wait_ge(gb_in, 64)
            for tile in range(TILES):
                for half in range(2):
                    groups = [(c, slice(512 * c, 512 * c + 512)) for c in (2 * half, 2 * half + 1)]
                    norm_columns([(result[:, tile, cols], acc[tile][c][:, :], P, tile, cols) for c, cols in groups],
                                 gb_last, ln_part)

        @block.gpsimd
        def _(pool):
            for n in range(len(loads)):
                if lo_by(n) == "pool":
                    pool.wait_ge(hi_done, n + 1)
                    split_rest(nc.gpsimd, n)

            nc.gpsimd.engine_nop().then_inc(u_free, SLOTS[0])
            nc.gpsimd.engine_nop().then_inc(hot_used, 2)
            nc.gpsimd.engine_nop().then_inc(grid_read, GRID_BANKS)
            ids_flat = ids[:, :, :].rearrange("p t n -> p (t n)")

            def gather(n, turn, k, slots):
                pool.wait_ge(u_free, n * OCT + (k + 1 + SLOTS[0] - slots))
                nc.gpsimd.sem_inc(slot_seen, 1)
                nc.gpsimd.indirect_dma_start(
                    out=U[k % slots][:, :], out_offset=None, in_=peer_u,
                    in_offset=bass.IndirectOffsetOnAxis(ap=idq[:, turn, k:k + 1], axis=0)
                ).then_inc(u_in[k % slots], 16)

            for tile in range(TILES):
                with pool.Fori(0, PARTS) as i:
                    part = i + tile * PARTS
                    pool.wait_ge(picks_ready, part + 1)
                    for turn in range(TURNS):
                        n = part * TURNS + turn
                        nc.gpsimd.tensor_copy(idq[:, turn, :], ids_flat[:, bass.ts(n, OCT)]).then_inc(ids_staged, 1)
                        pool.wait_ge(ids_staged, n + 1)
                        for k in range(OCT):
                            if tile == 0 and turn == 0 and k == 2:
                                pool.wait_ge(pj_full, PLAN.unit[("pq", 3, 3)] + 1)
                            gather(n, turn, k, SLOTS[tile])
                            if tile == 1:
                                if turn == 0 and k == 0:
                                    pool.wait_ge(turned_ready, 1)
                                    take_lot(nc.gpsimd, lot[0], lot_taken[0], i, i)
                                f = turn * (OCT // PAIR) + k // PAIR
                                if k % PAIR == 0:
                                    pool.wait_ge(hot_used, i * FILLS + f + 1)
                                    nc.gpsimd.sem_inc(slot_seen, 1)
                                fill_hot(nc.gpsimd, lot[0], hot[0][f % 2], f, (k % PAIR,), hot_full[0])
                    if tile == 1:
                        pool.wait_ge(hot_full[0], (i + 1) * FILLS)
                        nc.gpsimd.sem_inc(slot_seen, 1)
            pool.wait_ge(turned_ready, 2)
            with pool.Fori(0, ROUNDS) as i:
                take_lot(nc.gpsimd, lot[0], lot_taken[0], i + ROUNDS, i)
                for m, f in enumerate(POOL_FILLS):
                    pool.wait_ge(hot_used, i * FILLS + (2 + ROUNDS * FILLS - FILLS + f + 1))
                    nc.gpsimd.sem_inc(slot_seen, 1)
                    fill_hot(nc.gpsimd, lot[0], hot[0][m], f, range(PAIR), hot_full[0])
                pool.wait_ge(hot_full[0], i * len(POOL_FILLS) + (ROUNDS * FILLS + len(POOL_FILLS)))
                nc.gpsimd.sem_inc(slot_seen, 1)


def constants():
    import numpy as np
    f = np.float32
    c = np.zeros((P, C_END), f)
    for b, first in ((0, META), (1, META + P), (2, 0)):
        pos = (first + np.arange(P)).astype(f)
        for dh, o in ((AHD, C_ROPE_A), (RHD, C_ROPE_R)):
            inv = f(10000.0) ** (-np.arange(0, dh, 2, dtype=f) / f(dh))
            ang = (pos[:, None] * inv[None, :]).astype(f)
            w = dh // 2
            c[:, o + b * dh:o + b * dh + w] = np.cos(ang.astype(np.float64))
            c[:, o + b * dh + w:o + (b + 1) * dh] = np.sin(ang.astype(np.float64))
    i = np.arange(P)[:, None]
    for o, lo, keys, tile in ((C_MASK, 0, META + P, 0), (C_MASK + META + P, META, TOK, 1)):
        diff = (META + tile * P + i) - (lo + np.arange(keys)[None, :])
        c[:, o:o + keys] = np.where((diff >= 0) & (diff < 128), 0.0, NEG)
    q = np.arange(TOK)[None, :]
    for hd in range(RET_HEADS):
        g = 1.0 - 2.0 ** (-5.0 - hd)
        own = np.where(q - i >= 0, g ** np.maximum(q - i, 0).astype(np.float64), 0.0)
        met = g ** (q + META - i).astype(np.float64)
        o = C_DECAY + hd * 2 * TOK
        c[:, o:o + TOK] = own * RHD ** -0.5
        c[:, o + TOK:o + 2 * TOK] = met * RHD ** -0.5
    return c, np.eye(P, dtype=f), np.tile(np.arange(P, dtype=f), (P, 1))


def kernel(x, meta_tokens, ln_in_g, ln_in_b, w_in, att_sinks, w_out, ln_mix_g, ln_mix_b,
           peer_wq, peer_subkeys, peer_u, peer_v, ln_ffn_g, ln_ffn_b):
    import numpy as np
    import concourse.bacc as bacc
    from concourse.bass_utils import run_bass_kernel_spmd

    nc = bacc.Bacc("TRN2", target_bir_lowering=False, num_devices=1)
    consts, ident, iota = constants()
    given = {
        "x": np.asarray(x)[0], "meta": meta_tokens, "ln_in_g": ln_in_g, "ln_in_b": ln_in_b,
        "w_in": np.asarray(w_in)[0], "sinks": np.asarray(att_sinks)[0], "w_out": np.asarray(w_out)[0],
        "ln_mix_g": np.asarray(ln_mix_g)[0], "ln_mix_b": np.asarray(ln_mix_b)[0],
        "wq": np.asarray(peer_wq)[0],
        "subkeys": np.asarray(peer_subkeys)[0].reshape(2 * PH, NKEY, P).transpose(1, 0, 2),
        "peer_u": np.asarray(peer_u)[0], "peer_v": np.asarray(peer_v)[0],
        "ln_ffn_g": np.asarray(ln_ffn_g)[0], "ln_ffn_b": np.asarray(ln_ffn_b)[0],
        "consts": consts, "ident_c": ident, "iota_c": iota,
    }
    arrays, args = {}, []
    for name, value in given.items():
        arrays["in_" + name] = a = np.ascontiguousarray(value)
        args.append(nc.dram_tensor("in_" + name, a.shape, mybir.dt.from_np(a.dtype), kind="ExternalInput").ap())
    out = nc.dram_tensor("layer_out", (TOK, D), F32, kind="ExternalOutput").ap()
    build(nc, *args, out)
    r = run_bass_kernel_spmd(nc, [arrays], core_ids=[0])
    return np.asarray(r.results[0]["layer_out"]).reshape(1, TOK, D)
```
